# Optimizing a Trainium2 kernel written in Bass

```python
import jax, jax.numpy as jnp
from jax import lax
import numpy as np

D_MODEL = 1024
BATCH = 1
SEQ = 512
DEPTH = 2

CONV_CH = D_MODEL // 2
CONV_K = 3
SGU_WIDTH = D_MODEL // 2
SGU_GROUPS = 4
SGU_GROUP_CH = SGU_WIDTH // SGU_GROUPS
CHUNK = 128
ATT_HEADS = 8
HEAD_DIM = 64
ATT_WIDTH = ATT_HEADS * HEAD_DIM
Q_BLOCK = 128
N_BRANCH = 3
D_FF = ((8 * D_MODEL + 3 * 256 - 1) // (3 * 256)) * 256
IN_COLS = 3 * CONV_CH + 2 * SGU_WIDTH + 3 * ATT_WIDTH + N_BRANCH * D_MODEL
EPS = 1e-6

kernel_name = "hybrid_gated_conv_sgu_stickbreaking"

def _rmsnorm(x, g):
    xf = x.astype(jnp.float32)
    y = xf * lax.rsqrt(jnp.mean(xf * xf, axis=-1, keepdims=True) + EPS)
    return (y * g.astype(jnp.float32)).astype(x.dtype)

def _layernorm(x, g, b):
    xf = x.astype(jnp.float32)
    mu = jnp.mean(xf, axis=-1, keepdims=True)
    xc = xf - mu
    y = xc * lax.rsqrt(jnp.mean(xc * xc, axis=-1, keepdims=True) + EPS)
    return (y * g.astype(jnp.float32) + b.astype(jnp.float32)).astype(x.dtype)

def _split_cols(p):
    widths = (CONV_CH, CONV_CH, CONV_CH, SGU_WIDTH, SGU_WIDTH,
              ATT_WIDTH, ATT_WIDTH, ATT_WIDTH, N_BRANCH * D_MODEL)
    out, off = [], 0
    for w in widths:
        out.append(p[..., off:off + w])
        off += w
    return out

def _short_conv(bg, cg, xa, w, b):
    u = cg * xa
    S = u.shape[1]
    up = jnp.pad(u, ((0, 0), (CONV_K - 1, 0), (0, 0)))
    y = b
    for k in range(CONV_K):
        y = y + w[k] * up[:, k:k + S]
    return bg * y

def _sgu(u, v, ln_g, ln_b, w_s, b_s):
    u = jax.nn.gelu(u, approximate=False)
    v = _layernorm(jax.nn.gelu(v, approximate=False), ln_g, ln_b)
    B, S, _ = v.shape
    vc = v.reshape(B, S // CHUNK, CHUNK, SGU_GROUPS, SGU_GROUP_CH)
    causal = jnp.tril(jnp.ones((CHUNK, CHUNK), dtype=bool))
    w = jnp.where(causal[None], w_s, 0.0).astype(v.dtype)
    mixed = jnp.einsum('gts,bnsgc->bntgc', w, vc) + b_s.T[None, None, :, :, None]
    return u * mixed.reshape(B, S, SGU_WIDTH)

def _stick_breaking(q, k, v):
    B, H, S, d = q.shape
    nb = S // Q_BLOCK
    scale = 1.0 / float(np.sqrt(d))
    qb = q.reshape(B, H, nb, Q_BLOCK, d).transpose(2, 0, 1, 3, 4)
    key_pos = jnp.arange(S)

    def block(args):
        qi, i = args
        z = jnp.einsum('bhqd,bhkd->bhqk', qi, k).astype(jnp.float32) * scale
        qpos = i * Q_BLOCK + jnp.arange(Q_BLOCK)
        mask = key_pos[None, :] < qpos[:, None]
        log_beta = jax.nn.log_sigmoid(z)
        log_1m = jnp.where(mask, jax.nn.log_sigmoid(-z), 0.0)
        after = lax.cumsum(log_1m, axis=3, reverse=True) - log_1m
        a = jnp.where(mask, jnp.exp(log_beta + after), 0.0)
        return jnp.einsum('bhqk,bhkd->bhqd', a.astype(v.dtype), v)

    out = lax.map(block, (qb, jnp.arange(nb)))
    return out.transpose(1, 2, 0, 3, 4).reshape(B, H, S, d)

def setup_inputs(seed: int = 0) -> dict:
    key = jax.random.key(seed)
    ks = jax.random.split(key, 17)
    L, D = DEPTH, D_MODEL
    nrm = lambda k, shape, s: jax.random.normal(k, shape, jnp.float32) * s
    return {
        "x": jax.random.normal(ks[0], (BATCH, SEQ, D), jnp.float32),
        "mix_norm_g": 1.0 + nrm(ks[1], (L, D), 0.02),
        "w_in": nrm(ks[2], (L, D, IN_COLS), D ** -0.5),
        "b_gate": nrm(ks[3], (L, N_BRANCH * D), 0.02),
        "conv_w": nrm(ks[4], (L, CONV_K, CONV_CH), CONV_K ** -0.5),
        "conv_b": nrm(ks[5], (L, CONV_CH), 0.02),
        "sgu_ln_g": 1.0 + nrm(ks[6], (L, SGU_WIDTH), 0.02),
        "sgu_ln_b": nrm(ks[7], (L, SGU_WIDTH), 0.02),
        "sgu_w": nrm(ks[8], (L, SGU_GROUPS, CHUNK, CHUNK), CHUNK ** -0.5),
        "sgu_b": nrm(ks[9], (L, SGU_GROUPS, CHUNK), 0.02),
        "q_norm_g": 1.0 + nrm(ks[10], (L, HEAD_DIM), 0.02),
        "k_norm_g": 1.0 + nrm(ks[11], (L, HEAD_DIM), 0.02),
        "w_branch_out": nrm(ks[12], (L, N_BRANCH, CONV_CH, D), CONV_CH ** -0.5),
        "w_o": nrm(ks[13], (L, D, D), D ** -0.5),
        "ffn_norm_g": 1.0 + nrm(ks[14], (L, D), 0.02),
        "w_gate_up": nrm(ks[15], (L, D, 2 * D_FF), D ** -0.5),
        "w_down": nrm(ks[16], (L, D_FF, D), D_FF ** -0.5),
    }

def reference(x, mix_norm_g, w_in, b_gate, conv_w, conv_b, sgu_ln_g, sgu_ln_b, sgu_w, sgu_b,
              q_norm_g, k_norm_g, w_branch_out, w_o, ffn_norm_g, w_gate_up, w_down):
    B, S, D = x.shape
    for l in range(DEPTH):
        h = _rmsnorm(x, mix_norm_g[l])
        a_b, a_c, a_x, s_u, s_v, q, k, v, gates = _split_cols(h @ w_in[l])

        ya = _short_conv(a_b, a_c, a_x, conv_w[l], conv_b[l])
        yb = _sgu(s_u, s_v, sgu_ln_g[l], sgu_ln_b[l], sgu_w[l], sgu_b[l])

        qh = _rmsnorm(q.reshape(B, S, ATT_HEADS, HEAD_DIM), q_norm_g[l]).transpose(0, 2, 1, 3)
        kh = _rmsnorm(k.reshape(B, S, ATT_HEADS, HEAD_DIM), k_norm_g[l]).transpose(0, 2, 1, 3)
        vh = v.reshape(B, S, ATT_HEADS, HEAD_DIM).transpose(0, 2, 1, 3)
        yc = _stick_breaking(qh, kh, vh).transpose(0, 2, 1, 3).reshape(B, S, ATT_WIDTH)

        ys = jnp.stack([ya, yb, yc], axis=2)
        yd = jnp.einsum('bsnc,ncd->bsnd', ys, w_branch_out[l])
        g = jax.nn.sigmoid(gates + b_gate[l]).reshape(B, S, N_BRANCH, D)
        merged = jnp.sum(g * yd, axis=2)
        x = x + merged @ w_o[l]

        h2 = _rmsnorm(x, ffn_norm_g[l])
        gu = h2 @ w_gate_up[l]
        x = x + (jax.nn.silu(gu[..., :D_FF]) * gu[..., D_FF:]) @ w_down[l]
    return x


_drawn_inputs = setup_inputs


def setup_inputs(seed=0):
    import zlib

    import numpy as np

    out = dict(_drawn_inputs(seed))
    spreads = {}
    factors = {'b_gate': 7.976,
     'conv_b': 3.722,
     'sgu_ln_g': 8.0,
     'sgu_ln_b': 8.0,
     'sgu_b': 6.004,
     'q_norm_g': 8.0,
     'k_norm_g': 8.0,
     'ffn_norm_g': 2.938}
    for name, (base, spread) in spreads.items():
        noise = np.random.default_rng([zlib.crc32(name.encode()), seed]).standard_normal(out[name].shape)
        drawn = base * np.exp(spread * noise) if base else spread * noise
        out[name] = __import__('jax').numpy.asarray(drawn.astype(out[name].dtype))
    for name, factor in factors.items():
        out[name] = (out[name] * factor).astype(out[name].dtype)
    return out
```

```python
from contextlib import ExitStack

import concourse.bass as bass
from concourse import mybir

P = 128
T = 512
NT = T // P
D = 1024
KD = D // P
L = 2
CH = D // 2
KC = CH // P
HD = 64
PAIRS = CH // (2 * HD)
DFF = 2816
KF = DFF // P
PARTS = [(0, 8), (8, 8), (16, 6)]
EPS = 1e-6
MASKED = -1e30

C_B, C_C, C_X, C_U, C_SV, C_Q, C_K, C_V, C_G = [CH * i for i in range(8)] + [8 * CH]

RAW = 4
WS = 2
NB = 4

UP, UA, UM, UO = 10, 8 * 3 + 6, 4 * KD, KD
UF = [2 * n + KD for _, n in PARTS]
B_P, B_A, B_M, B_O = 0, UP, UP + UA, UP + UA + UM
B_F = [B_O + UO, B_O + UO + UF[0], B_O + UO + UF[0] + UF[1]]
UL = B_F[2] + UF[2]
assert UL % RAW == 0

R_GM, R_GF, R_BG, R_CW, R_CB, R_GQ, R_GK, NPAR = 0, 8, 16, 40, 52, 56, 57, 58

Z_BLOCKS = [(0, [0]), (1, [1, 3]), (2, [2])]
Z_AT = {0: 0, 1: 0, 3: 384, 2: 0}
S_AT = {0: 0, 1: 512, 3: 896, 2: 1024}
S_COLS = [(0, 512), (512, 512), (1024, 256)]

M_P, M_PAIR, M_PAIR_LAST = 8, 6, 3
M_LAYER = M_P + (PAIRS - 1) * M_PAIR + M_PAIR_LAST + 1
CHAINS = 2 + 2 * PAIRS

F32 = mybir.dt.float32
F32R = mybir.dt.float32r
ALU = mybir.AluOpType
ACT = mybir.ActivationFunctionType


class Units:

    def __init__(self, quad, off=0):
        self.quad, self.off = quad, off

    def count(self, c, credit=0):
        return self.quad * 4 + (self.off + c + 1 + credit)

    def round(self, c, step=1):
        return self.quad * step + ((self.off + c) // 4 + 1) * step

    def slot(self, c):
        return (self.off + c) % 4


def places(l):
    q = UL // 4
    return {
        "P": Units(l * q),
        "A": lambda j: Units(l * q + (B_A // 4) + j * 2, B_A % 4),
        "M": lambda m: Units(l * q + B_M // 4 + m),
        "O": lambda i: Units(l * q + B_O // 4 + i),
        "GU": lambda p, i: Units(l * q + B_F[p] // 4 + i),
        "WD": lambda p, i: Units(l * q + (B_F[p] + 2 * PARTS[p][1]) // 4 + i),
    }


def build(nc, x, mix_norm_g, w_in, b_gate, conv_w, conv_b, sgu_ln_g, sgu_ln_b, sgu_w, sgu_b,
          q_norm_g, k_norm_g, w_branch_out, w_o, ffn_norm_g, w_gate_up, w_down, out):
    ctx = ExitStack()
    with ctx:
        plan = [(nc.sbuf_base + 31) // 32 * 32]

        def sb(name, shape, dt=F32, at=None):
            size = 4
            for n in shape[1:]:
                size *= n
            if at is None:
                at = plan[0]
                plan[0] += (size + 31) // 32 * 32
            t = nc.alloc_sbuf_tensor_at(name, shape, dt, offset=at)
            offsets[name] = at
            return t

        offsets = {}

        def sem(name):
            return ctx.enter_context(nc.semaphore(name))

        xT = sb("xT", [P, KD, T])
        xg_hi = sb("xg_hi", [P, KD, T], F32R)
        xg_lo = sb("xg_lo", [P, KD, T], F32R)
        raw = [sb(f"raw{i}", [P, KD, P]) for i in range(RAW)]
        w_hi = [sb(f"w_hi{i}", [P, KD, P], F32R) for i in range(WS)]
        w_lo = [sb(f"w_lo{i}", [P, KD, P], F32R) for i in range(WS)]
        ident = sb("ident", [P, P])
        ones = sb("ones", [P, P])
        head_ones = sb("head_ones", [P, P])
        ident_r = sb("ident_r", [P, P], F32R)
        neg_tri = sb("neg_tri", [P, P], F32R)
        neg_ones = sb("neg_ones", [P, P], F32R)
        mask_add = sb("mask_add", [P, P], F32R)
        rstd = sb("rstd", [P, T])
        sgu_bias = sb("sgu_bias", [P, KC, P])
        sw_hi = sb("sw_hi", [P, KC, P], F32R)
        sw_lo = sb("sw_lo", [P, KC, P], F32R)
        eps = sb("eps", [P, 1])
        par_rows = sb("par_rows", [64, P])
        par = sb("par", [P, 64])
        gain0 = sb("gain0", [P, KD])
        ln_stats = sb("ln_stats", [P, NT, 6])
        ln_mv = sb("ln_mv", [P, NT, 2])
        ln_v = sb("ln_v", [P, NT])
        ln_r = sb("ln_r", [P, NT])
        ln_t = sb("ln_t", [P, NT])
        ln_rstd = sb("ln_rstd", [P, NT])
        ya_hi = sb("ya_hi", [P, KC, T], F32R)
        ya_lo = sb("ya_lo", [P, KC, T], F32R)
        yb_hi = sb("yb_hi", [P, KC, T], F32R)
        yb_lo = sb("yb_lo", [P, KC, T], F32R)
        yc_hi = sb("yc_hi", [P, KC, T], F32R)
        yc_lo = sb("yc_lo", [P, KC, T], F32R)
        v_tok = sb("v_tok", [P, NT, CH], at=offsets["yc_hi"])
        ln_g = sb("ln_g", [P, CH], at=offsets["yc_lo"])
        ln_b = sb("ln_b", [P, CH], at=offsets["yc_lo"] + 4 * CH)
        sw_raw = sb("sw_raw", [P, KC, P], at=offsets["yc_lo"] + 8 * CH)
        gates = sb("gates", [P, KD, T])
        toks = gates[:, :, :].rearrange("p a b -> p (a b)").rearrange("p (n d) -> p n d", n=NT)
        sq_sum = gates[:, 0, :]
        sq_one = gates[:, 1, :]
        S0 = sb("S0", [P, T])
        S1 = sb("S1", [P, T])
        S2 = sb("S2", [P, T])
        conv_in = sb("conv_in", [P, 2 + T])
        N0 = sb("N0", [P, T])
        N1 = sb("N1", [P, T])
        N2 = conv_in[:, 2:2 + T]
        over = plan[0]
        q_hi = sb("q_hi", [P, T], F32R)
        q_lo = sb("q_lo", [P, T], F32R)
        k_hi = sb("k_hi", [P, T], F32R)
        k_lo = sb("k_lo", [P, T], F32R)
        v_hi = sb("v_hi", [P, NT, P], F32R)
        v_lo = sb("v_lo", [P, NT, P], F32R)
        mix_hi = sb("mix_hi", [P, NT, P], F32R)
        mix_lo = sb("mix_lo", [P, NT, P], F32R)
        t_s = sb("t_s", [P, 1280])
        s_hi = sb("s_hi", [P, 1280], F32R)
        s_lo = sb("s_lo", [P, 1280], F32R)
        mid_hi = sb("mid_hi", [P, 8, T], F32R, at=over)
        mid_lo = sb("mid_lo", [P, 8, T], F32R, at=over + 8 * 4 * T)
        plan[0] = max(plan[0], over + 16 * 4 * T)
        assert plan[0] <= nc.sbuf_usable_end, plan[0]

        bank = [ctx.enter_context(nc.psum_tensor(f"bank{i}", [P, T], F32)) for i in range(NB)]
        z = [ctx.enter_context(nc.psum_tensor(f"z{i}", [P, T], F32)) for i in range(3)]
        misc = ctx.enter_context(nc.psum_tensor("misc", [P, T], F32))
        bank_yb, bank_sq = z[0], z[1]

        raw_full = [sem(f"raw_full{i}") for i in range(RAW)]
        hi_done = sem("hi_done")
        lo_done = sem("lo_done")
        hi_free = sem("hi_free")
        unit_done = sem("unit_done")
        bank_free = [sem(f"bank_free{i}") for i in range(NB)]
        passed = sem("passed")
        consts = sem("consts")
        ident_ok = sem("ident_ok")
        x_in = sem("x_in")
        par_in = sem("par_in")
        ln_in = sem("ln_in")
        sw_in = sem("sw_in")
        sw_masked = sem("sw_masked")
        par_ok = sem("par_ok")
        x_turned = sem("x_turned")
        x_new = sem("x_new")
        xg_hi_ok = sem("xg_hi_ok")
        xg_ok = sem("xg_ok")
        sq_ok = sem("sq_ok")
        sq_done = sem("sq_done")
        chain = sem("chain")
        chain_done = sem("chain_done")
        misc_done = sem("misc_done")
        misc_free = sem("misc_free")
        sv_raw = sem("sv_raw")
        sv_ok = sem("sv_ok")
        ln_var = sem("ln_var")
        ln_chain = sem("ln_chain")
        ln_pre = sem("ln_pre")
        ln_hi = sem("ln_hi")
        ln_ok = sem("ln_ok")
        sw_hi_ok = sem("sw_hi_ok")
        sw_ok = sem("sw_ok")
        qk_raw = sem("qk_raw")
        qk_sq = sem("qk_sq")
        qk_nrm = sem("qk_nrm")
        qk_hi = sem("qk_hi")
        qk_ok = sem("qk_ok")
        v_raw = sem("v_raw")
        v_hi_ok = sem("v_hi_ok")
        v_ok = sem("v_ok")
        slab_in = sem("slab_in")
        z_done = sem("z_done")
        z_ln = sem("z_ln")
        sp_ok = sem("sp_ok")
        sp_hi = sem("sp_hi")
        sp_lo = sem("sp_lo")
        cum_done = sem("cum_done")
        a_exp = sem("a_exp")
        a_lo = sem("a_lo")
        yc_hi_ok = sem("yc_hi_ok")
        yc_ok = sem("yc_ok")
        ya_pre = sem("ya_pre")
        ya_hi_ok = sem("ya_hi_ok")
        ya_ok = sem("ya_ok")
        u_raw = sem("u_raw")
        u_ok = sem("u_ok")
        yb_pre = sem("yb_pre")
        yb_hi_ok = sem("yb_hi_ok")
        yb_ok = sem("yb_ok")
        g_raw = sem("g_raw")
        g_sig = sem("g_sig")
        merged = sem("merged")
        yb_bank_free = sem("yb_bank_free")
        silu_in = sem("silu_in")
        silu_ok = sem("silu_ok")
        act_pre = sem("act_pre")
        mid_hi_ok = sem("mid_hi_ok")
        mid_ok = sem("mid_ok")
        o_turned = sem("o_turned")
        o_copied = sem("o_copied")
        stored = sem("stored")

        block = ctx.enter_context(nc.Block())

        @block.sync
        def _(sp):
            def cols(w, l, c0, r0=0, kc=KD):
                return w[l].rearrange("(c p) n -> p c n", p=P)[:, r0:r0 + kc, bass.ds(c0, P)]

            def load(at, c, src, kc=KD):
                sp.wait_ge(lo_done, at.count(c))
                sp.dma_start(raw[at.slot(c)][:, 0:kc, :], src).then_inc(raw_full[at.slot(c)], 16)

            sp.dma_start(toks, x.rearrange("b (n p) d -> p (b n) d", p=P)).then_inc(x_in, 16)
            sp.dma_start(par_rows[0:KD, :], mix_norm_g[0].rearrange("(a p) -> a p", p=P)).then_inc(x_in, 16)

            with sp.Fori(0, L) as l:
                pl = places(l)
                order = [C_SV, C_SV + P, C_SV + 2 * P, C_SV + 3 * P, C_Q, C_K] + [C_G + P * m for m in range(4, 8)]
                for c, c0 in enumerate(order):
                    load(pl["P"], c, cols(w_in, l, c0))
                    if c == 0:
                        sp.wait_ge(par_ok, l + 1)
                        sp.sem_inc(passed, 1)
                        rows = [(mix_norm_g[1 - l], R_GM, 8), (ffn_norm_g[l], R_GF, 8),
                                (b_gate[l], R_BG, 24), (conv_b[l], R_CB, 4)]
                        for src, r, n in rows:
                            sp.dma_start(par_rows[r:r + n, :], src.rearrange("(a p) -> a p", p=P)).then_inc(par_in, 16)
                        sp.dma_start(par_rows[R_CW:R_CW + 12, :],
                                     conv_w[l].rearrange("k (a p) -> (k a) p", p=P)).then_inc(par_in, 16)
                        for src, r in ((q_norm_g, R_GQ), (k_norm_g, R_GK)):
                            for h in range(2):
                                sp.dma_start(par_rows[r:r + 1, h * HD:(h + 1) * HD],
                                             src[l].rearrange("(a p) -> a p", a=1)).then_inc(par_in, 16)
                    if c == 1:
                        sp.dma_start(ln_g[:, :], sgu_ln_g[l].partition_broadcast(P)).then_inc(ln_in, 16)
                        sp.dma_start(ln_b[:, :], sgu_ln_b[l].partition_broadcast(P)).then_inc(ln_in, 16)
                        sp.dma_start(sgu_bias[:, :, :].rearrange("p g t -> p (g t)"),
                                     sgu_b[l].rearrange("g t -> (g t)").partition_broadcast(P)).then_inc(ln_in, 16)
                        sp.dma_start(sw_raw[:, :, :], sgu_w[l].rearrange("g t s -> t g s")).then_inc(sw_in, 16)

                def attention_loads(j, last):
                    at = pl["A"](j)
                    order = [C_V + P * j, C_B + P * j, C_C + P * j, C_X + P * j]
                    if not last:
                        order += [C_Q + P * (j + 1), C_K + P * (j + 1)]
                    order += [C_U + P * j, C_G + P * j]
                    for c, c0 in enumerate(order):
                        load(at, c, cols(w_in, l, c0))

                with sp.Fori(0, PAIRS - 1) as j:
                    attention_loads(j, False)
                attention_loads(PAIRS - 1, True)

                with sp.Fori(0, KD) as m:
                    at = pl["M"](m)
                    load(at, 0, cols(w_in, l, m * P + (C_G + D)))
                    load(at, 1, cols(w_in, l, m * P + (C_G + 2 * D)))
                    wb = w_branch_out[l].rearrange("n (c p) d -> p (n c) d", p=P)
                    load(at, 2, wb[:, 0:2 * KC, bass.ds(m * P, P)])
                    load(at, 3, wb[:, 2 * KC:3 * KC, bass.ds(m * P, P)], KC)

                with sp.Fori(0, 2) as i:
                    for c in range(4):
                        load(pl["O"](i), c, cols(w_o, l, i * (4 * P) + c * P))

                for p, (f0, n) in enumerate(PARTS):
                    with sp.Fori(0, n // 2) as i:
                        for c in range(4):
                            load(pl["GU"](p, i), c,
                                 cols(w_gate_up, l, i * (2 * P) + (f0 + c // 2) * P + (c % 2) * DFF))
                    r0 = min(f0, KF - KD)
                    with sp.Fori(0, 2) as i:
                        for c in range(4):
                            load(pl["WD"](p, i), c, cols(w_down, l, i * (4 * P) + c * P, r0))

            end = Units(L * UL // 4)
            for c in range(2):
                load(end, c, cols(w_o, 0, c * P))
            for n in range(NT):
                sp.wait_ge(o_copied, 2 * (n + 1))
                sp.dma_start(out[0, n * P:(n + 1) * P, :], toks[:, n, :]).then_inc(stored, 16)
            sp.wait_ge(stored, 16 * NT)

        @block.gpsimd
        def _(pool):
            def triangle(t, keep, fill, base, mult, step):
                nc.gpsimd.affine_select(out=t, in_=t, compare_op=keep, fill=fill, base=base,
                                        pattern=[[step, P]], channel_multiplier=mult)

            nc.gpsimd.memset(ident[:, :], 0.0)
            nc.gpsimd.memset(S0[:, 0:P], -1.0)
            nc.gpsimd.memset(S1[:, 0:P], 0.0)
            pool.drain()
            triangle(ident[:, :], ALU.not_equal, 1.0, 0, 1, -1)
            triangle(S0[:, 0:P], ALU.is_ge, 0.0, 0, 1, -1)
            triangle(S1[:, 0:P], ALU.is_gt, MASKED, 0, -1, 1)
            pool.drain()
            nc.gpsimd.memset(ones[:, :], 1.0).then_inc(ident_ok, 1)

            def square_sum(nth, c):
                pool.wait_ge(x_new, nth + 1)
                dst = sq_sum if c == 0 else sq_one
                nc.gpsimd.tensor_tensor(dst, xT[:, c, :], xT[:, c, :], ALU.mult)
                pool.drain()
                if c:
                    add = nc.gpsimd.tensor_tensor(sq_sum, sq_sum, sq_one, ALU.add)
                    if c == KD - 1:
                        add.then_inc(sq_ok, 1)
                    pool.drain()

            pool.wait_ge(x_new, KD)
            for c in range(KD):
                square_sum(c, c)
            with pool.Fori(0, L) as l:
                pool.wait_ge(sw_in, l * 16 + 16)
                pool.sem_inc(passed, 1)
                for g in range(KC):
                    last = nc.gpsimd.affine_select(
                        out=sw_raw[:, g, :], in_=sw_raw[:, g, :], compare_op=ALU.is_ge, fill=0.0,
                        base=0, pattern=[[-1, P]], channel_multiplier=1)
                last.then_inc(sw_masked, 1)
                for half in range(2):
                    for c in range(KD):
                        square_sum(l * (2 * KD) + (KD * (half + 1) + c), c)

        @block.tensor
        def _(pe):
            mm = nc.tensor.matmul

            def unit(at, c, his, los, dsts=None, kc=KD, k0=0, ready=None):
                wh, wl = w_hi[at.slot(c) % WS], w_lo[at.slot(c) % WS]
                dsts = dsts or [bank[at.slot(c)]]
                per = kc // len(dsts)
                pe.wait_ge(bank_free[at.slot(c)], at.round(c))
                pe.wait_ge(hi_done, at.count(c))
                for k in range(kc):
                    if ready:
                        pe.wait_ge(ready[0], ready[1] + (k + 1))
                    dst = dsts[k // per]
                    mm(dst[:, :], wh[:, k0 + k, :], his[k], start=(k % per == 0), stop=False)
                    last = mm(dst[:, :], wh[:, k0 + k, :], los[k], start=False, stop=False)
                last.then_inc(hi_free, 1)
                pe.wait_ge(lo_done, at.count(c, RAW))
                for k in range(kc):
                    last = mm(dsts[k // per][:, :], wl[:, k0 + k, :], his[k], start=False, stop=(k % per == per - 1))
                last.then_inc(unit_done, 1)

            xh = [xg_hi[:, k, :] for k in range(KD)]
            xl = [xg_lo[:, k, :] for k in range(KD)]

            def four_transposes(n_misc, src, what, value):
                pe.wait_ge(what, value)
                pe.wait_ge(misc_free, n_misc + 1)
                for n in range(4):
                    last = nc.tensor.transpose(misc[:, n * P:(n + 1) * P], src(n), ident[:, :])
                last.then_inc(misc_done, 1)

            def scores(h3, j_pairs, e):
                pe.wait_ge(a_exp, h3 + 3)
                pe.wait_ge(qk_ok, j_pairs * 2 + 2)
                rows = slice(HD * e, HD * e + HD)
                for g, blocks in Z_BLOCKS:
                    for n, i in enumerate(blocks):
                        dst = z[g][:, Z_AT[i]:Z_AT[i] + T - P * i]
                        ks, qs = slice(P * i, P * i + P), slice(P * i, T)
                        mm(dst, k_hi[rows, ks], q_hi[rows, qs], start=(n == 0), stop=False, skip_group_check=True)
                        mm(dst, k_hi[rows, ks], q_lo[rows, qs], start=False, stop=False, skip_group_check=True)
                        mm(dst, k_lo[rows, ks], q_hi[rows, qs], start=False, stop=False, skip_group_check=True)
                        last = mm(z[g][:, Z_AT[i]:Z_AT[i] + P], ident_r[:, :], mask_add[:, :],
                                  start=False, stop=True, skip_group_check=True)
                    last.then_inc(z_done, 1)

            def cumulate(h3):
                pe.wait_ge(sp_lo, h3 + 3)
                for g, blocks in Z_BLOCKS:
                    for i in blocks:
                        for i2 in range(i, NT):
                            width = T - P * i2
                            at = Z_AT[i] + P * (i2 - i)
                            w = neg_tri if i2 == i else neg_ones
                            for s in (s_hi, s_lo):
                                last = mm(z[g][:, at:at + width], w[:, :], s[:, S_AT[i2]:S_AT[i2] + width],
                                          start=False, stop=(i2 == NT - 1), skip_group_check=True)
                    last.then_inc(cum_done, 1)

            def attend(h3, n_misc, v_count):
                pe.wait_ge(a_lo, h3 + 3)
                pe.wait_ge(v_ok, v_count)
                pe.wait_ge(misc_free, n_misc + 1)
                for i in range(NT):
                    width = T - P * i
                    dst = misc[:, P * i:T]
                    a = slice(S_AT[i], S_AT[i] + width)
                    mm(dst, v_hi[:, i, :], s_hi[:, a], start=(i == 0), stop=False, skip_group_check=True)
                    mm(dst, v_hi[:, i, :], s_lo[:, a], start=False, stop=False, skip_group_check=True)
                    last = mm(dst, v_lo[:, i, :], s_hi[:, a], start=False, stop=(i == NT - 1), skip_group_check=True)
                last.then_inc(misc_done, 1)

            def head_squares(n_misc, nth):
                pe.wait_ge(qk_sq, nth)
                pe.wait_ge(misc_free, n_misc + 1)
                mm(misc[:, :], head_ones[:, :], S2[:, :], start=True, stop=True).then_inc(misc_done, 1)

            def row_squares(nth):
                pe.wait_ge(sq_ok, nth)
                mm(bank_sq[:, :], ones[:, :], sq_sum, start=True, stop=True).then_inc(sq_done, 1)

            def mix(n_misc, j, n_slab):
                pe.wait_ge(slab_in, n_slab)
                pe.wait_ge(misc_free, n_misc + 1)
                for n in range(NT):
                    dst = misc[:, n * P:(n + 1) * P]
                    wh = sw_hi[:, bass.ds(j, 1), :].rearrange("p a t -> p (a t)")
                    wl = sw_lo[:, bass.ds(j, 1), :].rearrange("p a t -> p (a t)")
                    mm(dst, mix_hi[:, n, :], wh, start=True, stop=False)
                    mm(dst, mix_hi[:, n, :], wl, start=False, stop=False)
                    last = mm(dst, mix_lo[:, n, :], wh, start=False, stop=True)
                last.then_inc(misc_done, 1)

            pe.wait_ge(x_in, 32)
            pe.wait_ge(ident_ok, 1)
            nc.tensor.transpose(misc[:, 0:KD], par_rows[0:KD, :], ident[0:KD, 0:KD]).then_inc(misc_done, 1)
            for c in range(KD):
                if c >= NB:
                    pe.wait_ge(x_new, c - NB + 1)
                for n in range(NT):
                    last = nc.tensor.transpose(bank[c % NB][:, n * P:(n + 1) * P], toks[:, n, c * P:(c + 1) * P],
                                               ident[:, :])
                last.then_inc(x_turned, 1)
            pe.wait_ge(x_new, KD)
            pe.wait_ge(consts, 1)

            with pe.Fori(0, L) as l:
                pl = places(l)
                m0 = l * M_LAYER + 1

                at = pl["P"]
                unit(at, 0, xh, xl, ready=(xg_ok, l * (2 * KD)))
                row_squares(l * 2 + 1)
                pe.wait_ge(par_in, l * (9 * 16) + 9 * 16)
                pe.wait_ge(misc_free, m0 + 1)
                pe.sem_inc(passed, 1)
                nc.tensor.transpose(misc[:, 0:NPAR], par_rows[0:NPAR, :], ident[0:NPAR, 0:NPAR]).then_inc(misc_done, 1)
                for c in range(1, 5):
                    unit(at, c, xh, xl)
                    s = (S0, S1)[(c - 1) % 2]
                    four_transposes(m0 + c, lambda n: s[:, n * P:(n + 1) * P], sv_ok, l * 4 + c)
                unit(at, 5, xh, xl)
                head_squares(m0 + 5, l * 8 + 1)
                unit(at, 6, xh, xl)
                head_squares(m0 + 6, l * 8 + 2)
                unit(at, 7, xh, xl)
                four_transposes(m0 + 7, lambda n: sw_raw[:, n, :], sw_masked, l + 1)
                unit(at, 8, xh, xl)
                unit(at, 9, xh, xl)
                m0 = m0 + M_P

                def pair(j, last, m0):
                    at = pl["A"](j)
                    h3 = l * 24 + j * 6
                    pairs = l * PAIRS + j
                    scores(h3, pairs, 0)
                    unit(at, 0, xh, xl)
                    unit(at, 1, xh, xl)
                    four_transposes(m0, lambda n: N0[:, n * P:(n + 1) * P], v_raw, pairs + 1)
                    cumulate(h3)
                    unit(at, 2, xh, xl)
                    unit(at, 3, xh, xl)
                    attend(h3, m0 + 1, pairs + 1)
                    scores(h3 + 3, pairs, 1)
                    unit(at, 4, xh, xl)
                    if last:
                        mix(m0 + 2, j, (pairs + 1) * 32)
                    else:
                        head_squares(m0 + 2, l * 8 + (j * 2 + 3))
                    unit(at, 5, xh, xl)
                    cumulate(h3 + 3)
                    if last:
                        return
                    head_squares(m0 + 3, l * 8 + (j * 2 + 4))
                    unit(at, 6, xh, xl)
                    mix(m0 + 4, j, (pairs + 1) * 32)
                    unit(at, 7, xh, xl)
                    attend(h3 + 3, m0 + 5, pairs + 1)

                with pe.Fori(0, PAIRS - 1) as j:
                    pair(j, False, m0 + j * M_PAIR)
                m0 = m0 + (PAIRS - 1) * M_PAIR
                pair(PAIRS - 1, True, m0)
                m0 = m0 + M_PAIR_LAST

                ybranch = [(ya_hi, ya_lo), (yb_hi, yb_lo)]
                abh = [h[:, k, :] for h, _ in ybranch for k in range(KC)]
                abl = [lo[:, k, :] for _, lo in ybranch for k in range(KC)]
                ch = [yc_hi[:, k, :] for k in range(KC)]
                cl = [yc_lo[:, k, :] for k in range(KC)]

                def merge(m, first):
                    at = pl["M"](m)
                    unit(at, 0, xh, xl)
                    unit(at, 1, xh, xl)
                    if first:
                        attend(l * 24 + 21, m0, (l + 1) * PAIRS)
                        pe.wait_ge(ya_ok, l * KC + KC)
                        pe.wait_ge(yb_ok, l * KC + KC)
                    pe.wait_ge(yb_bank_free, l * KD + m + 1)
                    unit(at, 2, abh, abl, [bank[at.slot(2)], bank_yb])
                    if first:
                        pe.wait_ge(yc_ok, l * 8 + 8)
                    unit(at, 3, ch, cl, kc=KC)

                merge(0, True)
                with pe.Fori(1, KD) as m:
                    merge(m, False)

                mh = [mid_hi[:, k, :] for k in range(8)]
                ml = [mid_lo[:, k, :] for k in range(8)]
                mids = l * (KD + KF)
                with pe.Fori(0, 2) as i:
                    for c in range(4):
                        unit(pl["O"](i), c, mh, ml, ready=(mid_ok, mids) if c == 0 else None)

                def gate_up(p, i, first=False):
                    at = pl["GU"](p, i)
                    for c in range(4):
                        unit(at, c, xh, xl, ready=(xg_ok, l * (2 * KD) + KD) if first and c == 0 else None)
                        if first and c == 0:
                            row_squares(l * 2 + 2)

                for p, (f0, n) in enumerate(PARTS):
                    if p == 0:
                        gate_up(0, 0, True)
                    with pe.Fori(1 if p == 0 else 0, n // 2) as i:
                        gate_up(p, i)
                    with pe.Fori(0, 2) as i:
                        for c in range(4):
                            unit(pl["WD"](p, i), c, mh[:n], ml[:n], kc=n, k0=KD - n,
                                 ready=(mid_ok, mids + (KD + f0)) if c == 0 else None)

            pe.wait_ge(x_new, KD + 2 * KD * L)
            for n in range(NT):
                for half in range(2):
                    b = 2 * n + half
                    if b >= NB:
                        pe.wait_ge(o_copied, b - NB + 1)
                    for c in range(4):
                        last = nc.tensor.transpose(bank[b % NB][:, c * P:(c + 1) * P],
                                                   xT[:, 4 * half + c, n * P:(n + 1) * P], ident[:, :])
                    last.then_inc(o_turned, 1)

        @block.scalar
        def _(act):
            af = nc.scalar.activation

            def split_hi(at, c, kc=KD):
                act.wait_ge(raw_full[at.slot(c)], at.round(c, 16))
                act.wait_ge(hi_free, at.count(c))
                act.wait_ge(lo_done, at.count(c, RAW - WS))
                af(w_hi[at.slot(c) % WS][:, 0:kc, :], raw[at.slot(c)][:, 0:kc, :], ACT.Copy).then_inc(hi_done, 1)

            def rms_chain(nth, src, count, freed=None):
                act.wait_ge(chain_done, nth + 1)
                op = af(N0[:, :], src[:, :], ACT.Identity, scale=1.0 / count, bias=eps[:, 0:1])
                if freed is not None:
                    op.then_inc(freed, 1)
                act.drain()
                af(N1[:, :], N0[:, :], ACT.Ln)
                act.drain()
                af(N1[:, :], N1[:, :], ACT.Exp, scale=-0.5)
                act.drain()
                af(N2, N1[:, :], ACT.Square).then_inc(chain, 1)

            def xg_round(n_new, c, gain):
                act.wait_ge(x_new, n_new)
                af(xg_hi[:, c, :], xT[:, c, :], ACT.Copy, scale=gain).then_inc(xg_hi_ok, 1)

            def softplus_logs(h3):
                for g, (a, n) in enumerate(S_COLS):
                    act.wait_ge(z_done, h3 + (g + 1))
                    af(t_s[:, a:a + n], z[g][:, 0:n], ACT.Abs)
                act.drain()
                for g, (a, n) in enumerate(S_COLS):
                    af(t_s[:, a:a + n], t_s[:, a:a + n], ACT.Exp, scale=-1.0)
                act.drain()
                for g, (a, n) in enumerate(S_COLS):
                    af(t_s[:, a:a + n], t_s[:, a:a + n], ACT.Ln, bias=1.0).then_inc(z_ln, 1)

            def softplus_hi(h3):
                for g, (a, n) in enumerate(S_COLS):
                    act.wait_ge(sp_ok, h3 + (g + 1))
                    af(s_hi[:, a:a + n], t_s[:, a:a + n], ACT.Copy).then_inc(sp_hi, 1)

            def attention_exp(h3):
                act.wait_ge(cum_done, h3 + 3)
                for g, (a, n) in enumerate(S_COLS):
                    af(s_hi[:, a:a + n], z[g][:, 0:n], ACT.Exp)
                    af(t_s[:, a:a + n], z[g][:, 0:n], ACT.Exp).then_inc(a_exp, 1)

            def yc_round(n_misc, j, e):
                rows = slice(HD * e, HD * e + HD)
                act.wait_ge(misc_done, n_misc + 1)
                af(yc_hi[rows, bass.ds(j, 1), :].rearrange("p a t -> p (a t)"), misc[rows, :], ACT.Copy).then_inc(yc_hi_ok, 1)

            def ln_round(l, n):
                act.wait_ge(ln_pre, l * NT + n + 1)
                af(yb_hi[:, :, n * P:(n + 1) * P], (S0, S1)[n % 2][:, :].rearrange("p (g c) -> p g c", g=KC),
                   ACT.Copy).then_inc(ln_hi, 1)

            act.wait_ge(consts, 1)
            start = Units(0)
            for c in range(2):
                split_hi(start, c)
            act.wait_ge(par_ok, 1)
            for c in range(KD):
                xg_round(c + 1, c, gain0[:, c:c + 1])

            with act.Fori(0, L) as l:
                pl = places(l)
                m0 = l * M_LAYER + 1
                at = pl["P"]
                nchain = l * CHAINS
                split_hi(at, 2)
                act.wait_ge(sq_done, l * 2 + 1)
                rms_chain(nchain, bank_sq, D)
                for c in range(4):
                    s = (S0, S1)[c % 2]
                    act.wait_ge(sv_raw, l * 4 + c + 1)
                    af(s[:, :], s[:, :], ACT.Gelu).then_inc(sv_ok, 1)
                    split_hi(at, 3 + c)
                act.wait_ge(qk_raw, l * 8 + 1)
                af(S2[:, :], S0[:, :], ACT.Square).then_inc(qk_sq, 1)
                split_hi(at, 7)
                act.wait_ge(misc_done, m0 + 6)
                act.wait_ge(qk_raw, l * 8 + 2)
                af(S2[:, :], S1[:, :], ACT.Square).then_inc(qk_sq, 1)
                rms_chain(nchain + 1, misc, HD, misc_free)
                act.wait_ge(ln_var, l + 1)
                af(ln_v[:, :], ln_mv[:, :, 1:2].rearrange("p n a -> p (n a)"), ACT.Identity, bias=eps[:, 0:1])
                act.drain()
                af(ln_r[:, :], ln_v[:, :], ACT.Ln)
                act.drain()
                af(ln_r[:, :], ln_r[:, :], ACT.Exp, scale=-0.5)
                act.drain()
                af(ln_t[:, :], ln_r[:, :], ACT.Square).then_inc(ln_chain, 1)
                split_hi(at, 8)
                act.wait_ge(qk_nrm, l * 8 + 1)
                af(q_hi[:, :], S0[:, :], ACT.Copy).then_inc(qk_hi, 1)
                act.wait_ge(misc_done, m0 + 7)
                rms_chain(nchain + 2, misc, HD, misc_free)
                act.wait_ge(qk_nrm, l * 8 + 2)
                af(k_hi[:, :], S1[:, :], ACT.Copy).then_inc(qk_hi, 1)
                split_hi(at, 9)
                act.wait_ge(misc_done, m0 + 8)
                af(sw_hi[:, :, :], misc[:, :].rearrange("p (g t) -> p g t", g=KC), ACT.Copy).then_inc(sw_hi_ok, 1)
                split_hi(at, 10)
                for n in range(2):
                    ln_round(l, n)
                split_hi(at, 11)
                for n in range(2, 4):
                    ln_round(l, n)
                m0 = m0 + M_P

                def pair(j, last, m0):
                    at = pl["A"](j)
                    h3 = l * 24 + j * 6
                    pairs = l * PAIRS + j
                    act.wait_ge(ln_ok, l * 4 + 4)
                    act.wait_ge(misc_done, m0 - 1)
                    for dst, src in ((mix_hi, yb_hi), (mix_lo, yb_lo)):
                        act.dma_start(dst[:, :, :].bitcast(F32),
                                      src[:, bass.ds(j, 1), :].rearrange("p a (n c) -> p (a n) c", n=NT).bitcast(F32)
                                      ).then_inc(slab_in, 16)
                    softplus_logs(h3)
                    split_hi(at, 2)
                    softplus_hi(h3)
                    split_hi(at, 3)
                    act.wait_ge(misc_done, m0 + 1)
                    af(v_hi[:, :, :], misc[:, :].rearrange("p (n c) -> p n c", n=NT), ACT.Copy).then_inc(v_hi_ok, 1)
                    attention_exp(h3)
                    split_hi(at, 4)
                    split_hi(at, 5)
                    yc_round(m0 + 1, j, 0)
                    act.wait_ge(ya_pre, pairs + 1)
                    af(ya_hi[:, bass.ds(j, 1), :].rearrange("p a t -> p (a t)"), S1[:, :], ACT.Copy).then_inc(ya_hi_ok, 1)
                    if last:
                        softplus_logs(h3 + 3)
                        split_hi(at, 6)
                        softplus_hi(h3 + 3)
                        act.wait_ge(u_raw, pairs + 1)
                        af(S2[:, :], S2[:, :], ACT.Gelu).then_inc(u_ok, 1)
                        act.wait_ge(yb_pre, pairs + 1)
                        af(yb_hi[:, bass.ds(j, 1), :].rearrange("p a t -> p (a t)"), S0[:, :], ACT.Copy).then_inc(yb_hi_ok, 1)
                        split_hi(at, 7)
                        attention_exp(h3 + 3)
                        return
                    softplus_logs(h3 + 3)
                    split_hi(at, 6)
                    act.wait_ge(qk_raw, l * 8 + (j * 2 + 3))
                    af(S2[:, :], S0[:, :], ACT.Square).then_inc(qk_sq, 1)
                    softplus_hi(h3 + 3)
                    split_hi(at, 7)
                    nch = l * CHAINS + (j * 2 + 3)
                    act.wait_ge(misc_done, m0 + 3)
                    act.wait_ge(qk_raw, l * 8 + (j * 2 + 4))
                    af(S2[:, :], S1[:, :], ACT.Square).then_inc(qk_sq, 1)
                    rms_chain(nch, misc, HD, misc_free)
                    attention_exp(h3 + 3)
                    act.wait_ge(qk_nrm, l * 8 + (j * 2 + 3))
                    af(q_hi[:, :], S0[:, :], ACT.Copy).then_inc(qk_hi, 1)
                    act.wait_ge(misc_done, m0 + 4)
                    rms_chain(nch + 1, misc, HD, misc_free)
                    split_hi(at, 8)
                    act.wait_ge(u_raw, pairs + 1)
                    af(S2[:, :], S2[:, :], ACT.Gelu).then_inc(u_ok, 1)
                    act.wait_ge(qk_nrm, l * 8 + (j * 2 + 4))
                    af(k_hi[:, :], S1[:, :], ACT.Copy).then_inc(qk_hi, 1)
                    split_hi(at, 9)
                    act.wait_ge(consts, 1)
                    act.wait_ge(yb_pre, pairs + 1)
                    af(yb_hi[:, bass.ds(j, 1), :].rearrange("p a t -> p (a t)"), S0[:, :], ACT.Copy).then_inc(yb_hi_ok, 1)
                    yc_round(m0 + 5, j, 1)

                with act.Fori(0, PAIRS - 1) as j:
                    pair(j, False, m0 + j * M_PAIR)
                m0 = m0 + (PAIRS - 1) * M_PAIR
                pair(PAIRS - 1, True, m0)
                m0 = m0 + M_PAIR_LAST

                act.wait_ge(yb_ok, l * KC + KC)
                act.wait_ge(par_ok, l + 2)

                def merge(m, first):
                    at = pl["M"](m)
                    nm = l * KD + m
                    split_hi(at, 2)
                    act.wait_ge(merged, nm + 1)
                    af(S0[:, :], gates[:, bass.ds(m, 1), :].rearrange("p a t -> p (a t)"), ACT.Sigmoid,
                       bias=par[:, bass.ds(m + R_BG, 1)]).then_inc(g_sig, 1)
                    split_hi(at, 3, KC)
                    act.wait_ge(g_raw, nm * 2 + 1)
                    af(S1[:, :], S1[:, :], ACT.Sigmoid, bias=par[:, bass.ds(m + (R_BG + KD), 1)]).then_inc(g_sig, 1)
                    if first:
                        yc_round(m0, PAIRS - 1, 1)
                    split_hi(at, 4)
                    act.wait_ge(g_raw, nm * 2 + 2)
                    af(S2[:, :], S2[:, :], ACT.Sigmoid, bias=par[:, bass.ds(m + (R_BG + 2 * KD), 1)]).then_inc(g_sig, 1)
                    split_hi(at, 5)
                    act.wait_ge(merged, nm + 2)
                    af(mid_hi[:, bass.ds(m, 1), :].rearrange("p a t -> p (a t)"), N0[:, :], ACT.Copy).then_inc(mid_hi_ok, 1)

                merge(0, True)
                with act.Fori(1, KD) as m:
                    merge(m, False)

                with act.Fori(0, 2) as i:
                    for c in range(4):
                        split_hi(pl["O"](i), c + 2)
                        xg_round(l * (2 * KD) + (i * 4 + (KD + c + 1)), bass.ds(i * 4 + c, 1),
                                 par[:, bass.ds(i * 4 + (R_GF + c), 1)])

                def gate_up(p, i, first=False):
                    at = pl["GU"](p, i)
                    f0 = PARTS[p][0]
                    for c in range(4):
                        f = i * 2 + c // 2
                        nf = l * KF + f0 + f
                        split_hi(at, c + 2)
                        if first and c == 0:
                            act.wait_ge(sq_done, l * 2 + 2)
                            rms_chain(l * CHAINS + (CHAINS - 1), bank_sq, D)
                        if c % 2 == 0:
                            act.wait_ge(silu_in, nf + 1)
                            af(S0[:, :], S0[:, :], ACT.Silu).then_inc(silu_ok, 1)
                        else:
                            act.wait_ge(act_pre, nf + 1)
                            af(mid_hi[:, bass.ds(f, 1), :].rearrange("p a t -> p (a t)"), N0[:, :], ACT.Copy
                               ).then_inc(mid_hi_ok, 1)

                for p, (f0, n) in enumerate(PARTS):
                    if p == 0:
                        gate_up(0, 0, True)
                    with act.Fori(1 if p == 0 else 0, n // 2) as i:
                        gate_up(p, i)
                    with act.Fori(0, 2) as i:
                        for c in range(4):
                            split_hi(pl["WD"](p, i), c + 2)
                            if p == len(PARTS) - 1:
                                xg_round(l * (2 * KD) + (i * 4 + (2 * KD + c + 1)), bass.ds(i * 4 + c, 1),
                                         par[:, bass.ds(i * 4 + (R_GM + c), 1)])

            act.wait_ge(sq_ok, 1 + 2 * L)
            for n in range(NT):
                act.wait_ge(o_turned, 2 * n + 1)
                if n:
                    act.wait_ge(o_copied, 2 * n)
                af(toks[:, n, 0:T], bank[(2 * n) % NB][:, :], ACT.Copy).then_inc(o_copied, 1)

        @block.vector
        def _(dve):
            tt, ts, stt = nc.vector.tensor_tensor, nc.vector.tensor_scalar, nc.vector.scalar_tensor_tensor
            copy = nc.vector.tensor_copy

            def split_lo(at, c, kc=KD):
                dve.wait_ge(hi_done, at.count(c))
                dve.wait_ge(unit_done, at.count(c))
                r, h, w = raw[at.slot(c)], w_hi[at.slot(c) % WS], w_lo[at.slot(c) % WS]
                tt(w[:, 0:kc, :], r[:, 0:kc, :], h[:, 0:kc, :].bitcast(F32), ALU.subtract).then_inc(lo_done, 1)

            def scaled(at, c, dst):
                dve.wait_ge(unit_done, at.count(c, 2))
                return tt(dst, bank[at.slot(c)][:, :], rstd[:, :], ALU.mult).then_inc(bank_free[at.slot(c)], 1)

            def newton(nth, dst):
                dve.wait_ge(chain, nth + 1)
                stt(N2, N0[:, :], -0.5, N2, ALU.mult, ALU.mult)
                dve.drain()
                stt(dst, N2, 1.5, N1[:, :], ALU.add, ALU.mult).then_inc(chain_done, 1)
                dve.drain()

            def xg_rest(n_hi, c, gain):
                dve.wait_ge(xg_hi_ok, n_hi)
                stt(xg_lo[:, c, :], xT[:, c, :], gain, xg_hi[:, c, :].bitcast(F32), ALU.mult, ALU.subtract
                    ).then_inc(xg_ok, 1)

            def softplus_sum(h3):
                for g, (a, n) in enumerate(S_COLS):
                    dve.wait_ge(z_ln, h3 + (g + 1))
                    stt(t_s[:, a:a + n], z[g][:, 0:n], 0.0, t_s[:, a:a + n], ALU.max, ALU.add).then_inc(sp_ok, 1)

            def softplus_lo(h3):
                for g, (a, n) in enumerate(S_COLS):
                    dve.wait_ge(sp_hi, h3 + (g + 1))
                    tt(s_lo[:, a:a + n], t_s[:, a:a + n], s_hi[:, a:a + n].bitcast(F32), ALU.subtract).then_inc(sp_lo, 1)

            def attention_lo(h3):
                for g, (a, n) in enumerate(S_COLS):
                    dve.wait_ge(a_exp, h3 + (g + 4))
                    tt(s_lo[:, a:a + n], t_s[:, a:a + n], s_hi[:, a:a + n].bitcast(F32), ALU.subtract).then_inc(a_lo, 1)

            def yc_rest(nth, j, e):
                rows = slice(HD * e, HD * e + HD)
                dve.wait_ge(yc_hi_ok, nth + 1)
                flat = lambda t: t[rows, bass.ds(j, 1), :].rearrange("p a t -> p (a t)")
                tt(flat(yc_lo), misc[rows, :], flat(yc_hi).bitcast(F32), ALU.subtract).then_inc(yc_ok, 1)
                dve.drain()
                dve.sem_inc(misc_free, 1)

            def head_norm(nth_chain, s, gain, n_qk):
                newton(nth_chain, N1[:, :])
                stt(s[:, :], s[:, :], gain, N1[:, :], ALU.mult, ALU.mult).then_inc(qk_nrm, 1)

            def head_rest(s, hi, lo, n_qk):
                dve.wait_ge(qk_hi, n_qk)
                tt(lo[:, :], s[:, :], hi[:, :].bitcast(F32), ALU.subtract).then_inc(qk_ok, 1)

            dve.sem_inc(lo_done, RAW)
            dve.sem_inc(hi_free, WS)
            dve.sem_inc(unit_done, WS)
            dve.sem_inc(a_exp, 3)
            dve.sem_inc(merged, 1)
            for s in (chain_done, misc_free, yb_bank_free):
                dve.sem_inc(s, 1)
            nc.vector.memset(eps[:, :], EPS)
            nc.vector.memset(conv_in[:, 0:2], 0.0)
            nc.vector.memset(head_ones[:, :], 0.0)
            nc.vector.memset(N0[:, 0:P], -1.0)
            dve.drain()
            nc.vector.memset(head_ones[0:HD, 0:HD], 1.0)
            nc.vector.memset(head_ones[HD:P, HD:P], 1.0)
            dve.wait_ge(ident_ok, 1)
            copy(ident_r[:, :], ident[:, :])
            copy(neg_tri[:, :], S0[:, 0:P])
            copy(mask_add[:, :], S1[:, 0:P])
            copy(neg_ones[:, :], N0[:, 0:P])
            dve.drain()
            dve.sem_inc(consts, 1)

            dve.wait_ge(misc_done, 1)
            copy(gain0[:, :], misc[:, 0:KD]).then_inc(par_ok, 1)
            dve.drain()
            dve.sem_inc(misc_free, 1)
            for c in range(KD):
                dve.wait_ge(x_turned, c + 1)
                copy(xT[:, c, :], bank[c % NB][:, :]).then_inc(x_new, 1)
                if c >= 1:
                    xg_rest(c, c - 1, gain0[:, c - 1:c])
            xg_rest(KD, KD - 1, gain0[:, KD - 1:KD])
            for b in range(NB):
                dve.sem_inc(bank_free[b], 1)
            start = Units(0)
            for c in range(2):
                split_lo(start, c)

            with dve.Fori(0, L) as l:
                pl = places(l)
                m0 = l * M_LAYER + 1
                at = pl["P"]
                nchain = l * CHAINS
                split_lo(at, 2)
                newton(nchain, rstd[:, :])
                scaled(at, 0, S0[:, :])
                dve.drain()
                dve.sem_inc(sv_raw, 1)
                dve.wait_ge(misc_done, m0 + 1)
                copy(par[:, 0:NPAR], misc[:, 0:NPAR])
                dve.drain()
                ts(par[:, R_GQ:R_GQ + 1], par[:, R_GQ:R_GQ + 1], HD ** -0.5, None, ALU.mult)
                dve.drain()
                dve.sem_inc(par_ok, 1)
                dve.sem_inc(misc_free, 1)
                for c in range(1, 5):
                    split_lo(at, 2 + c)
                    if c < 4:
                        scaled(at, c, (S0, S1)[c % 2][:, :])
                        dve.drain()
                        dve.sem_inc(sv_raw, 1)
                    else:
                        scaled(at, 4, S0[:, :])
                        dve.drain()
                        dve.sem_inc(qk_raw, 1)
                    dve.wait_ge(misc_done, m0 + c + 1)
                    copy(v_tok[:, :, (c - 1) * P:c * P], misc[:, :].rearrange("p (n c) -> p n c", n=NT)
                         ).then_inc(misc_free, 1)
                split_lo(at, 7)
                scaled(at, 5, S1[:, :])
                dve.drain()
                dve.sem_inc(qk_raw, 1)
                for n in range(NT):
                    nc.vector.bn_stats(ln_stats[:, n, :], v_tok[:, n, :])
                dve.drain()
                for n in range(NT):
                    nc.vector.bn_aggr(ln_mv[:, n, :], ln_stats[:, n, :])
                dve.drain()
                dve.sem_inc(ln_var, 1)
                head_norm(nchain + 1, S0, par[:, R_GQ:R_GQ + 1], l * 8 + 1)
                split_lo(at, 8)
                scaled(at, 6, gates[:, 4, :])
                head_rest(S0, q_hi, q_lo, l * 8 + 1)
                dve.wait_ge(ln_chain, l + 1)
                stt(ln_t[:, :], ln_v[:, :], -0.5, ln_t[:, :], ALU.mult, ALU.mult)
                dve.drain()
                stt(ln_rstd[:, :], ln_t[:, :], 1.5, ln_r[:, :], ALU.add, ALU.mult)
                dve.drain()
                head_norm(nchain + 2, S1, par[:, R_GK:R_GK + 1], l * 8 + 2)
                split_lo(at, 9)
                scaled(at, 7, gates[:, 5, :])
                head_rest(S1, k_hi, k_lo, l * 8 + 2)
                dve.wait_ge(sw_hi_ok, l + 1)
                tt(sw_lo[:, :, :], misc[:, :].rearrange("p (g t) -> p g t", g=KC), sw_hi[:, :, :].bitcast(F32),
                   ALU.subtract)
                dve.drain()
                dve.sem_inc(misc_free, 1)
                dve.wait_ge(ln_in, l * 48 + 48)
                for c in (8, 9):
                    split_lo(at, c + 2)
                    scaled(at, c, gates[:, c - 2, :])
                    for n in ((c - 8) * 2, (c - 8) * 2 + 1):
                        e = (S0, S1)[n % 2]
                        ts(e[:, :], v_tok[:, n, :], ln_mv[:, n, 0:1], ln_rstd[:, n:n + 1], ALU.subtract, ALU.mult)
                        dve.drain()
                        tt(e[:, :], e[:, :], ln_g[:, :], ALU.mult)
                        dve.drain()
                        tt(e[:, :], e[:, :], ln_b[:, :], ALU.add).then_inc(ln_pre, 1)
                        dve.wait_ge(ln_hi, l * 4 + n + 1)
                        tt(yb_lo[:, :, n * P:(n + 1) * P], e[:, :].rearrange("p (g c) -> p g c", g=KC),
                           yb_hi[:, :, n * P:(n + 1) * P].bitcast(F32), ALU.subtract).then_inc(ln_ok, 1)
                m0 = m0 + M_P

                def pair(j, last, m0):
                    at = pl["A"](j)
                    h3 = l * 24 + j * 6
                    pairs = l * PAIRS + j
                    j1 = bass.ds(j, 1)

                    def flat(t):
                        return t[:, j1, :].rearrange("p a t -> p (a t)")

                    softplus_sum(h3)
                    split_lo(at, 2)
                    scaled(at, 0, N0[:, :])
                    dve.drain()
                    dve.sem_inc(v_raw, 1)
                    softplus_lo(h3)
                    split_lo(at, 3)
                    scaled(at, 1, S0[:, :])
                    dve.wait_ge(v_hi_ok, pairs + 1)
                    tt(v_lo[:, :, :], misc[:, :].rearrange("p (n c) -> p n c", n=NT), v_hi[:, :, :].bitcast(F32),
                       ALU.subtract).then_inc(v_ok, 1)
                    dve.drain()
                    dve.sem_inc(misc_free, 1)
                    attention_lo(h3)
                    split_lo(at, 4)
                    scaled(at, 2, S1[:, :])
                    split_lo(at, 5)
                    scaled(at, 3, S2[:, :])
                    yc_rest(l * 8 + j * 2, j, 0)
                    tt(conv_in[:, 2:2 + T], S1[:, :], S2[:, :], ALU.mult)
                    dve.drain()

                    def tap(k):
                        return par[:, bass.ds(j + (R_CW + 4 * k), 1)]

                    ts(S1[:, :], conv_in[:, 2:2 + T], tap(2), par[:, bass.ds(j + R_CB, 1)], ALU.mult, ALU.add)
                    dve.drain()
                    stt(S1[:, :], conv_in[:, 1:1 + T], tap(1), S1[:, :], ALU.mult, ALU.add)
                    dve.drain()
                    stt(S1[:, :], conv_in[:, 0:T], tap(0), S1[:, :], ALU.mult, ALU.add)
                    dve.drain()
                    tt(S1[:, :], S1[:, :], S0[:, :], ALU.mult).then_inc(ya_pre, 1)
                    if last:
                        dve.wait_ge(ya_hi_ok, pairs + 1)
                        tt(flat(ya_lo), S1[:, :], flat(ya_hi).bitcast(F32), ALU.subtract).then_inc(ya_ok, 1)
                        softplus_sum(h3 + 3)
                        split_lo(at, 6)
                        scaled(at, 4, S2[:, :])
                        dve.drain()
                        dve.sem_inc(u_raw, 1)
                        softplus_lo(h3 + 3)
                        mixed(m0 + 2, j1, pairs, S0)
                        dve.wait_ge(yb_hi_ok, pairs + 1)
                        tt(flat(yb_lo), S0[:, :], flat(yb_hi).bitcast(F32), ALU.subtract).then_inc(yb_ok, 1)
                        split_lo(at, 7)
                        scaled(at, 5, flat(gates))
                        attention_lo(h3 + 3)
                        return
                    dve.wait_ge(ya_hi_ok, pairs + 1)
                    tt(flat(ya_lo), S1[:, :], flat(ya_hi).bitcast(F32), ALU.subtract).then_inc(ya_ok, 1)
                    softplus_sum(h3 + 3)
                    split_lo(at, 6)
                    scaled(at, 4, S0[:, :])
                    dve.drain()
                    dve.sem_inc(qk_raw, 1)
                    softplus_lo(h3 + 3)
                    split_lo(at, 7)
                    scaled(at, 5, S1[:, :])
                    dve.drain()
                    dve.sem_inc(qk_raw, 1)
                    nch = l * CHAINS + (j * 2 + 3)
                    head_norm(nch, S0, par[:, R_GQ:R_GQ + 1], None)
                    attention_lo(h3 + 3)
                    split_lo(at, 8)
                    head_rest(S0, q_hi, q_lo, l * 8 + (j * 2 + 3))
                    dve.wait_ge(misc_done, m0 + 4)
                    scaled(at, 6, S2[:, :])
                    dve.drain()
                    dve.sem_inc(u_raw, 1)
                    head_norm(nch + 1, S1, par[:, R_GK:R_GK + 1], None)
                    mixed(m0 + 4, j1, pairs, S0)
                    head_rest(S1, k_hi, k_lo, l * 8 + (j * 2 + 4))
                    split_lo(at, 9)
                    scaled(at, 7, flat(gates))
                    dve.wait_ge(yb_hi_ok, pairs + 1)
                    tt(flat(yb_lo), S0[:, :], flat(yb_hi).bitcast(F32), ALU.subtract).then_inc(yb_ok, 1)
                    yc_rest(l * 8 + (j * 2 + 1), j, 1)

                def mixed(n_misc, j1, pairs, dst):
                    dve.wait_ge(misc_done, n_misc + 1)
                    b = sgu_bias[:, j1, :].broadcast_to([P, NT, P])
                    tt(dst[:, :].rearrange("p (n t) -> p n t", n=NT), misc[:, :].rearrange("p (n t) -> p n t", n=NT),
                       b, ALU.add).then_inc(misc_free, 1)
                    dve.drain()
                    dve.wait_ge(u_ok, pairs + 1)
                    tt(dst[:, :], dst[:, :], S2[:, :], ALU.mult).then_inc(yb_pre, 1)

                with dve.Fori(0, PAIRS - 1) as j:
                    pair(j, False, m0 + j * M_PAIR)
                m0 = m0 + (PAIRS - 1) * M_PAIR
                pair(PAIRS - 1, True, m0)
                m0 = m0 + M_PAIR_LAST

                def merge(m, first):
                    at = pl["M"](m)
                    nm = l * KD + m
                    m1 = bass.ds(m, 1)
                    split_lo(at, 2)
                    scaled(at, 0, S1[:, :])
                    dve.drain()
                    dve.sem_inc(g_raw, 1)
                    split_lo(at, 3, KC)
                    scaled(at, 1, S2[:, :])
                    dve.drain()
                    dve.sem_inc(g_raw, 1)
                    if first:
                        yc_rest(l * 8 + 7, PAIRS - 1, 1)
                    split_lo(at, 4)
                    dve.wait_ge(g_sig, nm * 3 + 2)
                    dve.wait_ge(unit_done, at.count(2, 2))
                    tt(N0[:, :], bank[at.slot(2)][:, :], S0[:, :], ALU.mult).then_inc(bank_free[at.slot(2)], 1)
                    tt(N1[:, :], bank_yb[:, :], S1[:, :], ALU.mult).then_inc(yb_bank_free, 1)
                    dve.drain()
                    tt(N0[:, :], N0[:, :], N1[:, :], ALU.add)
                    split_lo(at, 5)
                    dve.drain()
                    dve.wait_ge(g_sig, nm * 3 + 3)
                    dve.wait_ge(unit_done, at.count(3, 2))
                    tt(N1[:, :], bank[at.slot(3)][:, :], S2[:, :], ALU.mult).then_inc(bank_free[at.slot(3)], 1)
                    dve.drain()
                    tt(N0[:, :], N0[:, :], N1[:, :], ALU.add).then_inc(merged, 1)
                    dve.wait_ge(mid_hi_ok, l * (KD + KF) + m + 1)
                    tt(mid_lo[:, m1, :].rearrange("p a t -> p (a t)"), N0[:, :],
                       mid_hi[:, m1, :].rearrange("p a t -> p (a t)").bitcast(F32), ALU.subtract).then_inc(mid_ok, 1)

                merge(0, True)
                with dve.Fori(1, KD) as m:
                    merge(m, False)

                def renew(at, c, i, prep, gain_row=0, news=0):
                    dve.wait_ge(unit_done, at.count(c, 2))
                    xc = bass.ds(i * 4 + c, 1)
                    xs = xT[:, xc, :].rearrange("p a t -> p (a t)")
                    tt(xs, xs, bank[at.slot(c)][:, :], ALU.add).then_inc(bank_free[at.slot(c)], 1)
                    if prep:
                        dve.drain()
                        dve.sem_inc(x_new, 1)
                        dve.wait_ge(xg_hi_ok, news + (i * 4 + (c + 1)))
                        stt(xg_lo[:, xc, :].rearrange("p a t -> p (a t)"), xs, par[:, bass.ds(i * 4 + (gain_row + c), 1)],
                            xg_hi[:, xc, :].rearrange("p a t -> p (a t)").bitcast(F32), ALU.mult, ALU.subtract
                            ).then_inc(xg_ok, 1)

                with dve.Fori(0, 2) as i:
                    at = pl["O"](i)
                    for c in range(4):
                        split_lo(at, c + 2)
                        renew(at, c, i, True, R_GF, l * (2 * KD) + KD)

                def gate_up(p, i, first=False):
                    at = pl["GU"](p, i)
                    f0 = PARTS[p][0]
                    for c in range(4):
                        f = i * 2 + c // 2
                        nf = l * KF + f0 + f
                        f1 = bass.ds(f, 1)
                        split_lo(at, c + 2)
                        if first and c == 0:
                            newton(l * CHAINS + (CHAINS - 1), rstd[:, :])
                        if c % 2 == 0:
                            scaled(at, c, S0[:, :])
                            dve.drain()
                            dve.sem_inc(silu_in, 1)
                        else:
                            scaled(at, c, S1[:, :])
                            dve.drain()
                            dve.wait_ge(silu_ok, nf + 1)
                            tt(N0[:, :], S0[:, :], S1[:, :], ALU.mult).then_inc(act_pre, 1)
                            dve.wait_ge(mid_hi_ok, l * (KD + KF) + (KD + f0) + f + 1)
                            tt(mid_lo[:, f1, :].rearrange("p a t -> p (a t)"), N0[:, :],
                               mid_hi[:, f1, :].rearrange("p a t -> p (a t)").bitcast(F32), ALU.subtract
                               ).then_inc(mid_ok, 1)

                for p, (f0, n) in enumerate(PARTS):
                    if p == 0:
                        gate_up(0, 0, True)
                    with dve.Fori(1 if p == 0 else 0, n // 2) as i:
                        gate_up(p, i)
                    with dve.Fori(0, 2) as i:
                        at = pl["WD"](p, i)
                        for c in range(4):
                            split_lo(at, c + 2)
                            renew(at, c, i, p == len(PARTS) - 1, R_GM, l * (2 * KD) + 2 * KD)

            dve.wait_ge(sq_ok, 1 + 2 * L)
            for n in range(NT):
                dve.wait_ge(o_turned, 2 * n + 2)
                dve.wait_ge(o_copied, 2 * n + 1)
                copy(toks[:, n, T:2 * T], bank[(2 * n + 1) % NB][:, :]).then_inc(o_copied, 1)


def kernel(**inputs):
    import numpy as np
    import concourse.bacc as bacc
    from concourse.bass_utils import run_bass_kernel_spmd

    names = ["x", "mix_norm_g", "w_in", "b_gate", "conv_w", "conv_b", "sgu_ln_g", "sgu_ln_b", "sgu_w", "sgu_b",
             "q_norm_g", "k_norm_g", "w_branch_out", "w_o", "ffn_norm_g", "w_gate_up", "w_down"]
    nc = bacc.Bacc("TRN2", target_bir_lowering=False, num_devices=1)
    arrays, args = {}, []
    for name in names:
        a = np.ascontiguousarray(inputs[name])
        arrays[f"in_{name}"] = a
        args.append(nc.dram_tensor(f"in_{name}", a.shape, mybir.dt.from_np(a.dtype), kind="ExternalInput").ap())
    out = nc.dram_tensor("out_x", (1, T, D), F32, kind="ExternalOutput").ap()
    build(nc, *args, out)
    got = run_bass_kernel_spmd(nc, [arrays], core_ids=[0])
    return got.results[0]["out_x"]
```

```python
from contextlib import ExitStack

import concourse.bass as bass
from concourse import mybir

P = 128
T = 512
NT = T // P
D = 1024
KD = D // P
L = 2
CH = D // 2
KC = CH // P
HD = 64
PAIRS = CH // (2 * HD)
DFF = 2816
KF = DFF // P
PARTS = [(0, 8), (8, 8), (16, 6)]
EPS = 1e-6
MASKED = -1e30

C_B, C_C, C_X, C_U, C_SV, C_Q, C_K, C_V, C_G = [CH * i for i in range(8)] + [8 * CH]

RAW = 4
AHEAD = 3
NB = 4

UP, UA, UM, UO = 10, 8 * 3 + 6, 4 * KD, KD
UF = [2 * n + KD for _, n in PARTS]
B_P, B_A, B_M, B_O = 0, UP, UP + UA, UP + UA + UM
B_F = [B_O + UO, B_O + UO + UF[0], B_O + UO + UF[0] + UF[1]]
UL = B_F[2] + UF[2]
assert UL % RAW == 0

R_GM, R_GF, R_BG, R_CW, R_CB, R_GQ, R_GK, NPAR = 0, 8, 16, 40, 52, 56, 57, 58

Z_BLOCKS = [(0, [0]), (1, [1, 3]), (2, [2])]
Z_AT = {0: 0, 1: 0, 3: 384, 2: 0}
S_AT = {0: 0, 1: 512, 3: 896, 2: 1024}
S_COLS = [(0, 512), (512, 512), (1024, 256)]

M_P, M_PAIR, M_PAIR_LAST = 5, 6, 3
M_LAYER = M_P + (PAIRS - 1) * M_PAIR + M_PAIR_LAST + 1
CHAINS = 2 + 2 * PAIRS

F32 = mybir.dt.float32
F32R = mybir.dt.float32r
ALU = mybir.AluOpType
ACT = mybir.ActivationFunctionType


class Units:

    def __init__(self, quad, off=0):
        self.quad, self.off = quad, off

    def count(self, c, credit=0):
        return self.quad * 4 + (self.off + c + 1 + credit)

    def round(self, c, step=1):
        return self.quad * step + ((self.off + c) // 4 + 1) * step

    def slot(self, c):
        return (self.off + c) % 4


def places(l):
    q = UL // 4
    return {
        "P": Units(l * q),
        "A": lambda j: Units(l * q + (B_A // 4) + j * 2, B_A % 4),
        "M": lambda m: Units(l * q + B_M // 4 + m),
        "O": lambda i: Units(l * q + B_O // 4 + i),
        "GU": lambda p, i: Units(l * q + B_F[p] // 4 + i),
        "WD": lambda p, i: Units(l * q + (B_F[p] + 2 * PARTS[p][1]) // 4 + i),
    }


def build(nc, x, mix_norm_g, w_in, b_gate, conv_w, conv_b, sgu_ln_g, sgu_ln_b, sgu_w, sgu_b,
          q_norm_g, k_norm_g, w_branch_out, w_o, ffn_norm_g, w_gate_up, w_down, out):
    ctx = ExitStack()
    with ctx:
        plan = [(nc.sbuf_base + 31) // 32 * 32]

        def sb(name, shape, dt=F32, at=None):
            size = 4
            for n in shape[1:]:
                size *= n
            if at is None:
                at = plan[0]
                plan[0] += (size + 31) // 32 * 32
            t = nc.alloc_sbuf_tensor_at(name, shape, dt, offset=at)
            offsets[name] = at
            return t

        offsets = {}

        def sem(name):
            return ctx.enter_context(nc.semaphore(name))

        xT = sb("xT", [P, KD, T])
        xg_hi = sb("xg_hi", [P, KD, T], F32R)
        xg_lo = sb("xg_lo", [P, KD, T], F32R)
        raw = [sb(f"raw{i}", [P, KD, P]) for i in range(RAW)]
        w_lo = [sb(f"w_lo{i}", [P, KD, P], F32R, at=offsets[f"raw{i}"]) for i in range(RAW)]
        w_hi = [sb(f"w_hi{i}", [P, KD, P], F32R) for i in range(RAW)]
        ident = sb("ident", [P, P])
        ones = sb("ones", [P, P])
        head_ones = sb("head_ones", [P, P])
        ident_r = sb("ident_r", [P, P], F32R)
        neg_tri = sb("neg_tri", [P, P], F32R)
        neg_ones = sb("neg_ones", [P, P], F32R)
        mask_add = sb("mask_add", [P, P], F32R)
        rstd = sb("rstd", [P, T])
        sgu_bias = sb("sgu_bias", [P, KC, P])
        sw_hi = sb("sw_hi", [P, KC, P], F32R)
        sw_lo = sb("sw_lo", [P, KC, P], F32R)
        eps = sb("eps", [P, 1])
        par_rows = sb("par_rows", [64, P])
        par = sb("par", [P, 64])
        gain0 = sb("gain0", [P, KD])
        ln_stats = sb("ln_stats", [P, NT, 6])
        ln_mv = sb("ln_mv", [P, NT, 2])
        ln_v = sb("ln_v", [P, NT])
        ln_r = sb("ln_r", [P, NT])
        ln_t = sb("ln_t", [P, NT])
        ln_rstd = sb("ln_rstd", [P, NT])
        ya_hi = sb("ya_hi", [P, KC, T], F32R)
        ya_lo = sb("ya_lo", [P, KC, T], F32R)
        yb_hi = sb("yb_hi", [P, KC, T], F32R)
        yb_lo = sb("yb_lo", [P, KC, T], F32R)
        yc_hi = sb("yc_hi", [P, KC, T], F32R)
        yc_lo = sb("yc_lo", [P, KC, T], F32R)
        v_tok = sb("v_tok", [P, NT, CH], at=offsets["yc_hi"])
        ln_g = sb("ln_g", [P, CH], at=offsets["yc_lo"])
        ln_b = sb("ln_b", [P, CH], at=offsets["yc_lo"] + 4 * CH)
        sw_raw = sb("sw_raw", [P, KC, P], at=offsets["yc_lo"] + 8 * CH)
        gates = sb("gates", [P, KD, T])
        toks = gates[:, :, :].rearrange("p a b -> p (a b)").rearrange("p (n d) -> p n d", n=NT)
        S0 = sb("S0", [P, T])
        S1 = sb("S1", [P, T])
        S2 = sb("S2", [P, T])
        QT = sb("QT", [P, T])
        KT = sb("KT", [P, T])
        conv_in = sb("conv_in", [P, 2 + T])
        N0 = sb("N0", [P, T])
        N1 = sb("N1", [P, T])
        N2 = conv_in[:, 2:2 + T]
        sq_sum, sq_one = S2[:, :], N1[:, :]
        over = plan[0]
        q_hi = sb("q_hi", [P, T], F32R)
        q_lo = sb("q_lo", [P, T], F32R)
        k_hi = sb("k_hi", [P, T], F32R)
        k_lo = sb("k_lo", [P, T], F32R)
        v_hi = sb("v_hi", [P, NT, P], F32R)
        v_lo = sb("v_lo", [P, NT, P], F32R)
        mix_hi = sb("mix_hi", [P, NT, P], F32R)
        mix_lo = sb("mix_lo", [P, NT, P], F32R)
        t_s = sb("t_s", [P, 1280])
        s_hi = sb("s_hi", [P, 1280], F32R)
        s_lo = sb("s_lo", [P, 1280], F32R)
        mid_hi = sb("mid_hi", [P, 8, T], F32R, at=over)
        mid_lo = sb("mid_lo", [P, 8, T], F32R, at=over + 8 * 4 * T)
        plan[0] = max(plan[0], over + 16 * 4 * T)
        assert plan[0] <= nc.sbuf_usable_end, plan[0]

        bank = [ctx.enter_context(nc.psum_tensor(f"bank{i}", [P, T], F32)) for i in range(NB)]
        z = [ctx.enter_context(nc.psum_tensor(f"z{i}", [P, T], F32)) for i in range(3)]
        misc = ctx.enter_context(nc.psum_tensor("misc", [P, T], F32))
        bank_yb, bank_sq = z[0], z[1]
        sv_bank = [z[0], z[2], z[1]]

        raw_full = [sem(f"raw_full{i}") for i in range(RAW)]
        hi_done = sem("hi_done")
        lo_done = sem("lo_done")
        unit_done = sem("unit_done")
        bank_free = [sem(f"bank_free{i}") for i in range(NB)]
        passed = sem("passed")
        consts = sem("consts")
        ident_ok = sem("ident_ok")
        x_in = sem("x_in")
        par_in = sem("par_in")
        ln_in = sem("ln_in")
        sw_in = sem("sw_in")
        sw_masked = sem("sw_masked")
        par_ok = sem("par_ok")
        x_turned = sem("x_turned")
        x_new = sem("x_new")
        xg_hi_ok = sem("xg_hi_ok")
        xg_ok = sem("xg_ok")
        sq_ok = sem("sq_ok")
        sq_done = sem("sq_done")
        chain = sem("chain")
        chain_done = sem("chain_done")
        misc_done = sem("misc_done")
        misc_free = sem("misc_free")
        sv_raw = sem("sv_raw")
        sv_ok = sem("sv_ok")
        sv_turned = sem("sv_turned")
        ln_var = sem("ln_var")
        ln_chain = sem("ln_chain")
        ln_pre = sem("ln_pre")
        ln_hi = sem("ln_hi")
        ln_ok = sem("ln_ok")
        sw_hi_ok = sem("sw_hi_ok")
        sw_ok = sem("sw_ok")
        qk_raw = sem("qk_raw")
        qk_sq = sem("qk_sq")
        qk_nrm = sem("qk_nrm")
        qk_hi = sem("qk_hi")
        qk_ok = sem("qk_ok")
        v_raw = sem("v_raw")
        v_hi_ok = sem("v_hi_ok")
        v_ok = sem("v_ok")
        slab_in = sem("slab_in")
        z_done = sem("z_done")
        z_ln = sem("z_ln")
        sp_ok = sem("sp_ok")
        sp_hi = sem("sp_hi")
        sp_lo = sem("sp_lo")
        cum_done = sem("cum_done")
        a_exp = sem("a_exp")
        a_hi = sem("a_hi")
        a_lo = sem("a_lo")
        yc_hi_ok = sem("yc_hi_ok")
        yc_ok = sem("yc_ok")
        ya_pre = sem("ya_pre")
        ya_hi_ok = sem("ya_hi_ok")
        ya_ok = sem("ya_ok")
        u_raw = sem("u_raw")
        u_ok = sem("u_ok")
        yb_pre = sem("yb_pre")
        yb_hi_ok = sem("yb_hi_ok")
        yb_ok = sem("yb_ok")
        g_raw = sem("g_raw")
        g_sig = sem("g_sig")
        merged = sem("merged")
        yb_bank_free = sem("yb_bank_free")
        silu_in = sem("silu_in")
        silu_ok = sem("silu_ok")
        act_pre = sem("act_pre")
        mid_hi_ok = sem("mid_hi_ok")
        mid_ok = sem("mid_ok")
        o_turned = sem("o_turned")
        o_act = sem("o_act")
        o_dve = sem("o_dve")
        stored = sem("stored")

        block = ctx.enter_context(nc.Block())

        @block.sync
        def _(sp):
            def cols(w, l, c0, r0=0, kc=KD):
                return w[l].rearrange("(c p) n -> p c n", p=P)[:, r0:r0 + kc, bass.ds(c0, P)]

            def load(at, c, src, kc=KD):
                sp.wait_ge(unit_done, at.count(c))
                sp.dma_start(raw[at.slot(c)][:, 0:kc, :], src).then_inc(raw_full[at.slot(c)], 16)

            sp.dma_start(toks, x.rearrange("b (n p) d -> p (b n) d", p=P)).then_inc(x_in, 16)
            sp.dma_start(par_rows[0:KD, :], mix_norm_g[0].rearrange("(a p) -> a p", p=P)).then_inc(x_in, 16)

            with sp.Fori(0, L) as l:
                pl = places(l)
                order = [C_SV, C_SV + P, C_SV + 2 * P, C_SV + 3 * P, C_Q, C_K] + [C_G + P * m for m in range(4, 8)]
                for c, c0 in enumerate(order):
                    load(pl["P"], c, cols(w_in, l, c0))
                    if c == 0:
                        sp.wait_ge(par_ok, l + 1)
                        sp.sem_inc(passed, 1)
                        rows = [(mix_norm_g[1 - l], R_GM, 8), (ffn_norm_g[l], R_GF, 8),
                                (b_gate[l], R_BG, 24), (conv_b[l], R_CB, 4)]
                        for src, r, n in rows:
                            sp.dma_start(par_rows[r:r + n, :], src.rearrange("(a p) -> a p", p=P)).then_inc(par_in, 16)
                        sp.dma_start(par_rows[R_CW:R_CW + 12, :],
                                     conv_w[l].rearrange("k (a p) -> (k a) p", p=P)).then_inc(par_in, 16)
                        for src, r in ((q_norm_g, R_GQ), (k_norm_g, R_GK)):
                            for h in range(2):
                                sp.dma_start(par_rows[r:r + 1, h * HD:(h + 1) * HD],
                                             src[l].rearrange("(a p) -> a p", a=1)).then_inc(par_in, 16)
                    if c == 1:
                        sp.dma_start(ln_g[:, :], sgu_ln_g[l].partition_broadcast(P)).then_inc(ln_in, 16)
                        sp.dma_start(ln_b[:, :], sgu_ln_b[l].partition_broadcast(P)).then_inc(ln_in, 16)
                        sp.dma_start(sgu_bias[:, :, :].rearrange("p g t -> p (g t)"),
                                     sgu_b[l].rearrange("g t -> (g t)").partition_broadcast(P)).then_inc(ln_in, 16)
                        sp.dma_start(sw_raw[:, :, :], sgu_w[l].rearrange("g t s -> t g s")).then_inc(sw_in, 16)

                def attention_loads(j, last):
                    at = pl["A"](j)
                    order = [C_V + P * j]
                    if not last:
                        order += [C_Q + P * (j + 1), C_K + P * (j + 1)]
                    order += [C_B + P * j, C_C + P * j, C_X + P * j, C_U + P * j, C_G + P * j]
                    for c, c0 in enumerate(order):
                        load(at, c, cols(w_in, l, c0))

                with sp.Fori(0, PAIRS - 1) as j:
                    attention_loads(j, False)
                attention_loads(PAIRS - 1, True)

                with sp.Fori(0, KD) as m:
                    at = pl["M"](m)
                    load(at, 0, cols(w_in, l, m * P + (C_G + D)))
                    load(at, 1, cols(w_in, l, m * P + (C_G + 2 * D)))
                    wb = w_branch_out[l].rearrange("n (c p) d -> p (n c) d", p=P)
                    load(at, 2, wb[:, 0:2 * KC, bass.ds(m * P, P)])
                    load(at, 3, wb[:, 2 * KC:3 * KC, bass.ds(m * P, P)], KC)

                with sp.Fori(0, 2) as i:
                    for c in range(4):
                        load(pl["O"](i), c, cols(w_o, l, i * (4 * P) + c * P))

                for p, (f0, n) in enumerate(PARTS):
                    with sp.Fori(0, n // 2) as i:
                        for c in range(4):
                            load(pl["GU"](p, i), c,
                                 cols(w_gate_up, l, i * (2 * P) + (f0 + c // 2) * P + (c % 2) * DFF))
                    r0 = min(f0, KF - KD)
                    with sp.Fori(0, 2) as i:
                        for c in range(4):
                            load(pl["WD"](p, i), c, cols(w_down, l, i * (4 * P) + c * P, r0))

            end = Units(L * UL // 4)
            for c in range(AHEAD):
                load(end, c, cols(w_o, 0, c * P))
            for n in range(NT):
                sp.wait_ge(o_act, n + 1)
                sp.wait_ge(o_dve, n + 1)
                sp.dma_start(out[0, n * P:(n + 1) * P, :], toks[:, n, :]).then_inc(stored, 16)
            sp.wait_ge(stored, 16 * NT)

        @block.gpsimd
        def _(pool):
            def triangle(t, keep, fill, base, mult, step):
                nc.gpsimd.affine_select(out=t, in_=t, compare_op=keep, fill=fill, base=base,
                                        pattern=[[step, P]], channel_multiplier=mult)

            nc.gpsimd.memset(ident[:, :], 0.0)
            nc.gpsimd.memset(S0[:, 0:P], -1.0)
            nc.gpsimd.memset(S1[:, 0:P], 0.0)
            pool.drain()
            triangle(ident[:, :], ALU.not_equal, 1.0, 0, 1, -1)
            triangle(S0[:, 0:P], ALU.is_ge, 0.0, 0, 1, -1)
            triangle(S1[:, 0:P], ALU.is_gt, MASKED, 0, -1, 1)
            pool.drain()
            nc.gpsimd.memset(ones[:, :], 1.0).then_inc(ident_ok, 1)

            def square_sum(nth, c):
                pool.wait_ge(x_new, nth + 1)
                dst = sq_sum if c == 0 else sq_one
                nc.gpsimd.tensor_tensor(dst, xT[:, c, :], xT[:, c, :], ALU.mult)
                pool.drain()
                if c:
                    add = nc.gpsimd.tensor_tensor(sq_sum, sq_sum, sq_one, ALU.add)
                    if c == KD - 1:
                        add.then_inc(sq_ok, 1)
                    pool.drain()

            def head_square(nth, src, n_misc=None):
                pool.wait_ge(qk_raw, nth)
                if n_misc is not None:
                    pool.wait_ge(misc_done, n_misc)
                    pool.sem_inc(passed, 1)
                nc.gpsimd.tensor_tensor(S2[:, :], src[:, :], src[:, :], ALU.mult).then_inc(qk_sq, 1)

            for c in range(KD):
                square_sum(c, c)
            with pool.Fori(0, L) as l:
                pool.wait_ge(sw_in, l * 16 + 16)
                pool.sem_inc(passed, 1)
                for g in range(KC):
                    last = nc.gpsimd.affine_select(
                        out=sw_raw[:, g, :], in_=sw_raw[:, g, :], compare_op=ALU.is_ge, fill=0.0,
                        base=0, pattern=[[-1, P]], channel_multiplier=1)
                last.then_inc(sw_masked, 1)
                m0 = l * M_LAYER + 1
                head_square(l * 8 + 1, QT)
                head_square(l * 8 + 2, KT, m0 + 3)
                with pool.Fori(0, PAIRS - 1) as j:
                    m = m0 + j * M_PAIR + M_P
                    head_square(l * 8 + (j * 2 + 3), QT)
                    head_square(l * 8 + (j * 2 + 4), KT, m + 2)
                for half in range(2):
                    for c in range(KD):
                        square_sum(l * (2 * KD) + (KD * (half + 1) + c), c)

        @block.tensor
        def _(pe):
            mm = nc.tensor.matmul

            def unit(at, c, his, los, dsts=None, kc=KD, k0=0, ready=None):
                wh, wl = w_hi[at.slot(c)], w_lo[at.slot(c)]
                dsts = dsts or [bank[at.slot(c)]]
                per = kc // len(dsts)

                def w_hi_passes(k):
                    if ready:
                        pe.wait_ge(ready[0], ready[1] + (k + 1))
                    dst = dsts[k // per]
                    mm(dst[:, :], wh[:, k0 + k, :], his[k], start=(k % per == 0), stop=False)
                    mm(dst[:, :], wh[:, k0 + k, :], los[k], start=False, stop=False)

                def w_lo_pass(k):
                    return mm(dsts[k // per][:, :], wl[:, k0 + k, :], his[k], start=False, stop=(k % per == per - 1))

                pe.wait_ge(bank_free[at.slot(c)], at.round(c))
                pe.wait_ge(hi_done, at.count(c))
                late = 1 if ready else 0
                for k in range(kc - late):
                    w_hi_passes(k)
                pe.wait_ge(lo_done, at.count(c))
                for k in range(kc - late):
                    last = w_lo_pass(k)
                if late:
                    w_hi_passes(kc - 1)
                    last = w_lo_pass(kc - 1)
                last.then_inc(unit_done, 1)

            xh = [xg_hi[:, k, :] for k in range(KD)]
            xl = [xg_lo[:, k, :] for k in range(KD)]

            def turn(dst, src):
                for n in range(4):
                    last = nc.tensor.transpose(dst[:, n * P:(n + 1) * P], src(n), ident[:, :])
                return last

            def four_transposes(n_misc, src, what, value):
                pe.wait_ge(what, value)
                pe.wait_ge(misc_free, n_misc + 1)
                turn(misc, src).then_inc(misc_done, 1)

            def scores(h3, j_pairs, e):
                pe.wait_ge(a_exp, h3 + 3)
                pe.wait_ge(qk_ok, j_pairs * 2 + 2)
                rows = slice(HD * e, HD * e + HD)
                for g, blocks in Z_BLOCKS:
                    for n, i in enumerate(blocks):
                        dst = z[g][:, Z_AT[i]:Z_AT[i] + T - P * i]
                        ks, qs = slice(P * i, P * i + P), slice(P * i, T)
                        mm(dst, k_hi[rows, ks], q_hi[rows, qs], start=(n == 0), stop=False, skip_group_check=True)
                        mm(dst, k_hi[rows, ks], q_lo[rows, qs], start=False, stop=False, skip_group_check=True)
                        mm(dst, k_lo[rows, ks], q_hi[rows, qs], start=False, stop=False, skip_group_check=True)
                        last = mm(z[g][:, Z_AT[i]:Z_AT[i] + P], ident_r[:, :], mask_add[:, :],
                                  start=False, stop=True, skip_group_check=True)
                    last.then_inc(z_done, 1)

            def cumulate(h3):
                pe.wait_ge(sp_lo, h3 + 3)
                for g, blocks in Z_BLOCKS:
                    for i in blocks:
                        for i2 in range(i, NT):
                            width = T - P * i2
                            at = Z_AT[i] + P * (i2 - i)
                            w = neg_tri if i2 == i else neg_ones
                            for s in (s_hi, s_lo):
                                last = mm(z[g][:, at:at + width], w[:, :], s[:, S_AT[i2]:S_AT[i2] + width],
                                          start=False, stop=(i2 == NT - 1), skip_group_check=True)
                    last.then_inc(cum_done, 1)

            def attend(h3, n_misc, v_count):
                pe.wait_ge(a_lo, h3 + 3)
                pe.wait_ge(v_ok, v_count)
                pe.wait_ge(misc_free, n_misc + 1)
                for i in range(NT):
                    width = T - P * i
                    dst = misc[:, P * i:T]
                    a = slice(S_AT[i], S_AT[i] + width)
                    mm(dst, v_hi[:, i, :], s_hi[:, a], start=(i == 0), stop=False, skip_group_check=True)
                    mm(dst, v_hi[:, i, :], s_lo[:, a], start=False, stop=False, skip_group_check=True)
                    last = mm(dst, v_lo[:, i, :], s_hi[:, a], start=False, stop=(i == NT - 1), skip_group_check=True)
                last.then_inc(misc_done, 1)

            def head_squares(n_misc, nth):
                pe.wait_ge(qk_sq, nth)
                pe.wait_ge(misc_free, n_misc + 1)
                mm(misc[:, :], head_ones[:, :], S2[:, :], start=True, stop=True).then_inc(misc_done, 1)

            def row_squares(nth):
                pe.wait_ge(sq_ok, nth)
                mm(bank_sq[:, :], ones[:, :], sq_sum, start=True, stop=True).then_inc(sq_done, 1)

            def mix(n_misc, j, n_slab):
                pe.wait_ge(slab_in, n_slab)
                pe.wait_ge(misc_free, n_misc + 1)
                for n in range(NT):
                    dst = misc[:, n * P:(n + 1) * P]
                    wh = sw_hi[:, bass.ds(j, 1), :].rearrange("p a t -> p (a t)")
                    wl = sw_lo[:, bass.ds(j, 1), :].rearrange("p a t -> p (a t)")
                    mm(dst, mix_hi[:, n, :], wh, start=True, stop=False)
                    mm(dst, mix_hi[:, n, :], wl, start=False, stop=False)
                    last = mm(dst, mix_lo[:, n, :], wh, start=False, stop=True)
                last.then_inc(misc_done, 1)

            pe.wait_ge(x_in, 32)
            pe.wait_ge(ident_ok, 1)
            nc.tensor.transpose(misc[:, 0:KD], par_rows[0:KD, :], ident[0:KD, 0:KD]).then_inc(misc_done, 1)
            for c in range(KD):
                if c >= NB:
                    pe.wait_ge(x_new, c - NB + 1)
                for n in range(NT):
                    last = nc.tensor.transpose(bank[c % NB][:, n * P:(n + 1) * P], toks[:, n, c * P:(c + 1) * P],
                                               ident[:, :])
                last.then_inc(x_turned, 1)
            pe.wait_ge(x_new, KD)
            pe.wait_ge(consts, 1)

            with pe.Fori(0, L) as l:
                pl = places(l)
                m0 = l * M_LAYER + 1

                at = pl["P"]
                unit(at, 0, xh, xl, ready=(xg_ok, l * (2 * KD)))
                unit(at, 1, xh, xl)
                row_squares(l * 2 + 1)
                unit(at, 2, xh, xl)
                pe.wait_ge(par_in, l * (9 * 16) + 9 * 16)
                pe.wait_ge(misc_free, m0 + 1)
                pe.sem_inc(passed, 1)
                nc.tensor.transpose(misc[:, 0:NPAR], par_rows[0:NPAR, :], ident[0:NPAR, 0:NPAR]).then_inc(misc_done, 1)
                unit(at, 3, xh, xl)
                unit(at, 4, xh, xl)
                for c in range(3):
                    pe.wait_ge(sv_ok, l * 4 + c + 1)
                    turn(sv_bank[c], lambda n: gates[:, c, n * P:(n + 1) * P]).then_inc(sv_turned, 1)
                unit(at, 5, xh, xl)
                four_transposes(m0 + 1, lambda n: gates[:, 3, n * P:(n + 1) * P], sv_ok, l * 4 + 4)
                unit(at, 6, xh, xl)
                head_squares(m0 + 2, l * 8 + 1)
                unit(at, 7, xh, xl)
                head_squares(m0 + 3, l * 8 + 2)
                unit(at, 8, xh, xl)
                four_transposes(m0 + 4, lambda n: sw_raw[:, n, :], sw_masked, l + 1)
                unit(at, 9, xh, xl)
                m0 = m0 + M_P

                def pair(j, last, m0):
                    at = pl["A"](j)
                    h3 = l * 24 + j * 6
                    pairs = l * PAIRS + j
                    scores(h3, pairs, 0)
                    unit(at, 0, xh, xl)
                    unit(at, 1, xh, xl)
                    four_transposes(m0, lambda n: N0[:, n * P:(n + 1) * P], v_raw, pairs + 1)
                    unit(at, 2, xh, xl)
                    cumulate(h3)
                    if last:
                        unit(at, 3, xh, xl)
                        attend(h3, m0 + 1, pairs + 1)
                        scores(h3 + 3, pairs, 1)
                        unit(at, 4, xh, xl)
                        mix(m0 + 2, j, (pairs + 1) * 32)
                        unit(at, 5, xh, xl)
                        return
                    head_squares(m0 + 1, l * 8 + (j * 2 + 3))
                    unit(at, 3, xh, xl)
                    attend(h3, m0 + 2, pairs + 1)
                    scores(h3 + 3, pairs, 1)
                    unit(at, 4, xh, xl)
                    head_squares(m0 + 3, l * 8 + (j * 2 + 4))
                    unit(at, 5, xh, xl)
                    mix(m0 + 4, j, (pairs + 1) * 32)
                    unit(at, 6, xh, xl)
                    cumulate(h3 + 3)
                    unit(at, 7, xh, xl)
                    attend(h3 + 3, m0 + 5, pairs + 1)

                with pe.Fori(0, PAIRS - 1) as j:
                    pair(j, False, m0 + j * M_PAIR)
                m0 = m0 + (PAIRS - 1) * M_PAIR
                pair(PAIRS - 1, True, m0)
                m0 = m0 + M_PAIR_LAST

                ybranch = [(ya_hi, ya_lo), (yb_hi, yb_lo)]
                abh = [h[:, k, :] for h, _ in ybranch for k in range(KC)]
                abl = [lo[:, k, :] for _, lo in ybranch for k in range(KC)]
                ch = [yc_hi[:, k, :] for k in range(KC)]
                cl = [yc_lo[:, k, :] for k in range(KC)]

                def merge(m, first):
                    at = pl["M"](m)
                    unit(at, 0, xh, xl)
                    if first:
                        cumulate(l * 24 + 21)
                    unit(at, 1, xh, xl)
                    if first:
                        attend(l * 24 + 21, m0, (l + 1) * PAIRS)
                        pe.wait_ge(ya_ok, l * KC + KC)
                        pe.wait_ge(yb_ok, l * KC + KC)
                    pe.wait_ge(yb_bank_free, l * KD + m + 1)
                    unit(at, 2, abh, abl, [bank[at.slot(2)], bank_yb])
                    if first:
                        pe.wait_ge(yc_ok, l * 8 + 8)
                    unit(at, 3, ch, cl, kc=KC)

                merge(0, True)
                with pe.Fori(1, KD) as m:
                    merge(m, False)

                mh = [mid_hi[:, k, :] for k in range(8)]
                ml = [mid_lo[:, k, :] for k in range(8)]
                mids = l * (KD + KF)
                with pe.Fori(0, 2) as i:
                    for c in range(4):
                        unit(pl["O"](i), c, mh, ml, ready=(mid_ok, mids) if c == 0 else None)

                def gate_up(p, i, first=False):
                    at = pl["GU"](p, i)
                    for c in range(4):
                        unit(at, c, xh, xl, ready=(xg_ok, l * (2 * KD) + KD) if first and c == 0 else None)
                        if first and c == 1:
                            row_squares(l * 2 + 2)

                for p, (f0, n) in enumerate(PARTS):
                    if p == 0:
                        gate_up(0, 0, True)
                    with pe.Fori(1 if p == 0 else 0, n // 2) as i:
                        gate_up(p, i)
                    with pe.Fori(0, 2) as i:
                        for c in range(4):
                            unit(pl["WD"](p, i), c, mh[:n], ml[:n], kc=n, k0=KD - n,
                                 ready=(mid_ok, mids + (KD + f0)) if c == 0 else None)

            pe.wait_ge(x_new, KD + 2 * KD * L)
            for n in range(NT):
                for half in range(2):
                    b = 2 * n + half
                    if b >= NB:
                        pe.wait_ge((o_act, o_dve)[half], n - 1)
                    for c in range(4):
                        last = nc.tensor.transpose(bank[b % NB][:, c * P:(c + 1) * P],
                                                   xT[:, 4 * half + c, n * P:(n + 1) * P], ident[:, :])
                    last.then_inc(o_turned, 1)

        @block.scalar
        def _(act):
            af = nc.scalar.activation

            def split_hi(at, c, kc=KD):
                act.wait_ge(raw_full[at.slot(c)], at.round(c, 16))
                af(w_hi[at.slot(c)][:, 0:kc, :], raw[at.slot(c)][:, 0:kc, :], ACT.Copy).then_inc(hi_done, 1)

            def rms_chain(nth, src, count, freed=None):
                act.wait_ge(chain_done, nth + 1)
                op = af(N0[:, :], src[:, :], ACT.Identity, scale=1.0 / count, bias=eps[:, 0:1])
                if freed is not None:
                    op.then_inc(freed, 1)
                act.drain()
                af(N1[:, :], N0[:, :], ACT.Ln)
                act.drain()
                af(N1[:, :], N1[:, :], ACT.Exp, scale=-0.5)
                act.drain()
                af(N2, N1[:, :], ACT.Square).then_inc(chain, 1)

            def xg_round(n_new, c, gain):
                act.wait_ge(x_new, n_new)
                af(xg_hi[:, c, :], xT[:, c, :], ACT.Copy, scale=gain).then_inc(xg_hi_ok, 1)

            def ln_exp_table():
                act.preload_act_table_set("natural_log_exp_and_others")

            def softplus_logs(h3):
                for g, (a, n) in enumerate(S_COLS):
                    act.wait_ge(z_done, h3 + (g + 1))
                    af(t_s[:, a:a + n], z[g][:, 0:n], ACT.Abs)
                act.drain()
                for g, (a, n) in enumerate(S_COLS):
                    af(t_s[:, a:a + n], t_s[:, a:a + n], ACT.Exp, scale=-1.0)
                act.drain()
                for g, (a, n) in enumerate(S_COLS):
                    af(t_s[:, a:a + n], t_s[:, a:a + n], ACT.Ln, bias=1.0).then_inc(z_ln, 1)

            def softplus_hi(h3):
                for g, (a, n) in enumerate(S_COLS):
                    act.wait_ge(sp_ok, h3 + (g + 1))
                    af(s_hi[:, a:a + n], t_s[:, a:a + n], ACT.Copy).then_inc(sp_hi, 1)

            def attention_exp(h3):
                for g, (a, n) in enumerate(S_COLS):
                    act.wait_ge(cum_done, h3 + (g + 1))
                    af(t_s[:, a:a + n], z[g][:, 0:n], ACT.Exp).then_inc(a_exp, 1)
                act.drain()
                for g, (a, n) in enumerate(S_COLS):
                    af(s_hi[:, a:a + n], t_s[:, a:a + n], ACT.Copy).then_inc(a_hi, 1)

            def yc_round(n_misc, j, e):
                rows = slice(HD * e, HD * e + HD)
                act.wait_ge(misc_done, n_misc + 1)
                af(yc_hi[rows, bass.ds(j, 1), :].rearrange("p a t -> p (a t)"), misc[rows, :], ACT.Copy).then_inc(yc_hi_ok, 1)

            def ln_round(l, n):
                act.wait_ge(ln_pre, l * NT + n + 1)
                af(yb_hi[:, :, n * P:(n + 1) * P], (S0, S1)[n % 2][:, :].rearrange("p (g c) -> p g c", g=KC),
                   ACT.Copy).then_inc(ln_hi, 1)

            act.wait_ge(consts, 1)
            start = Units(0)
            for c in range(AHEAD):
                split_hi(start, c)
            act.wait_ge(par_ok, 1)
            for c in range(KD):
                xg_round(c + 1, c, gain0[:, c:c + 1])

            with act.Fori(0, L) as l:
                pl = places(l)
                m0 = l * M_LAYER + 1
                at = pl["P"]
                nchain = l * CHAINS
                split_hi(at, 3)
                split_hi(at, 4)
                ln_exp_table()
                act.wait_ge(sq_done, l * 2 + 1)
                rms_chain(nchain, bank_sq, D)
                for c in range(4):
                    act.wait_ge(sv_raw, l * 4 + c + 1)
                    af(gates[:, c, :], gates[:, c, :], ACT.Gelu).then_inc(sv_ok, 1)
                    if c >= 2:
                        split_hi(at, 3 + c)
                split_hi(at, 7)
                split_hi(at, 8)
                ln_exp_table()
                act.wait_ge(ln_var, l + 1)
                af(ln_v[:, :], ln_mv[:, :, 1:2].rearrange("p n a -> p (n a)"), ACT.Identity, bias=eps[:, 0:1])
                act.drain()
                af(ln_r[:, :], ln_v[:, :], ACT.Ln)
                act.drain()
                af(ln_r[:, :], ln_r[:, :], ACT.Exp, scale=-0.5)
                act.drain()
                af(ln_t[:, :], ln_r[:, :], ACT.Square).then_inc(ln_chain, 1)
                act.wait_ge(misc_done, m0 + 3)
                rms_chain(nchain + 1, misc, HD, misc_free)
                split_hi(at, 9)
                act.wait_ge(qk_nrm, l * 8 + 1)
                af(q_hi[:, :], QT[:, :], ACT.Copy).then_inc(qk_hi, 1)
                act.wait_ge(misc_done, m0 + 4)
                rms_chain(nchain + 2, misc, HD, misc_free)
                ln_round(l, 0)
                split_hi(at, 10)
                act.wait_ge(qk_nrm, l * 8 + 2)
                af(k_hi[:, :], KT[:, :], ACT.Copy).then_inc(qk_hi, 1)
                ln_round(l, 1)
                split_hi(at, 11)
                act.wait_ge(misc_done, m0 + 5)
                af(sw_hi[:, :, :], misc[:, :].rearrange("p (g t) -> p g t", g=KC), ACT.Copy).then_inc(sw_hi_ok, 1)
                for n in range(2, 4):
                    ln_round(l, n)
                split_hi(at, 12)
                m0 = m0 + M_P

                def pair(j, last, m0):
                    at = pl["A"](j)
                    h3 = l * 24 + j * 6
                    pairs = l * PAIRS + j

                    def flat(t):
                        return t[:, bass.ds(j, 1), :].rearrange("p a t -> p (a t)")

                    def mix_slabs():
                        act.wait_ge(ln_ok, l * 4 + 4)
                        act.wait_ge(misc_done, m0 - 1)
                        for dst, src in ((mix_hi, yb_hi), (mix_lo, yb_lo)):
                            act.dma_start(dst[:, :, :].bitcast(F32),
                                          src[:, bass.ds(j, 1), :].rearrange("p a (n c) -> p (a n) c", n=NT).bitcast(F32)
                                          ).then_inc(slab_in, 16)

                    def ya_round():
                        act.wait_ge(ya_pre, pairs + 1)
                        af(flat(ya_hi), S1[:, :], ACT.Copy).then_inc(ya_hi_ok, 1)

                    def gelu_u():
                        act.wait_ge(u_raw, pairs + 1)
                        af(S2[:, :], S2[:, :], ACT.Gelu).then_inc(u_ok, 1)

                    def yb_round():
                        act.wait_ge(yb_pre, pairs + 1)
                        act.sem_inc(passed, 1)
                        af(flat(yb_hi), N0[:, :], ACT.Copy).then_inc(yb_hi_ok, 1)

                    softplus_logs(h3)
                    softplus_hi(h3)
                    split_hi(at, 3)
                    mix_slabs()
                    split_hi(at, 4)
                    act.wait_ge(misc_done, m0 + 1)
                    af(v_hi[:, :, :], misc[:, :].rearrange("p (n c) -> p n c", n=NT), ACT.Copy).then_inc(v_hi_ok, 1)
                    split_hi(at, 5)
                    attention_exp(h3)
                    if last:
                        split_hi(at, 6)
                        yc_round(m0 + 1, j, 0)
                        softplus_logs(h3 + 3)
                        split_hi(at, 7)
                        softplus_hi(h3 + 3)
                        ya_round()
                        split_hi(at, 8)
                        gelu_u()
                        yb_round()
                        ln_exp_table()
                        return
                    nch = l * CHAINS + (j * 2 + 3)
                    act.wait_ge(misc_done, m0 + 2)
                    rms_chain(nch, misc, HD, misc_free)
                    split_hi(at, 6)
                    yc_round(m0 + 2, j, 0)
                    softplus_logs(h3 + 3)
                    act.wait_ge(qk_nrm, l * 8 + (j * 2 + 3))
                    af(q_hi[:, :], QT[:, :], ACT.Copy).then_inc(qk_hi, 1)
                    split_hi(at, 7)
                    softplus_hi(h3 + 3)
                    act.wait_ge(misc_done, m0 + 4)
                    rms_chain(nch + 1, misc, HD, misc_free)
                    split_hi(at, 8)
                    act.wait_ge(qk_nrm, l * 8 + (j * 2 + 4))
                    af(k_hi[:, :], KT[:, :], ACT.Copy).then_inc(qk_hi, 1)
                    ya_round()
                    split_hi(at, 9)
                    attention_exp(h3 + 3)
                    gelu_u()
                    split_hi(at, 10)
                    yb_round()
                    ln_exp_table()
                    yc_round(m0 + 5, j, 1)

                ln_exp_table()
                with act.Fori(0, PAIRS - 1) as j:
                    pair(j, False, m0 + j * M_PAIR)
                m0 = m0 + (PAIRS - 1) * M_PAIR
                pair(PAIRS - 1, True, m0)
                m0 = m0 + M_PAIR_LAST

                act.wait_ge(ya_ok, l * KC + KC)
                act.wait_ge(par_ok, l + 2)

                def merge(m, first):
                    at = pl["M"](m)
                    nm = l * KD + m

                    def sigmoid(s, gate, bias):
                        af(s[:, :], gate, ACT.Sigmoid, bias=par[:, bass.ds(m + (R_BG + bias * KD), 1)]).then_inc(g_sig, 1)

                    split_hi(at, 3, KC)
                    if first:
                        split_hi(at, 4)
                        attention_exp(l * 24 + 21)
                    act.wait_ge(merged, nm + 1)
                    sigmoid(S0, gates[:, bass.ds(m, 1), :].rearrange("p a t -> p (a t)"), 0)
                    act.wait_ge(g_raw, nm * 2 + 1)
                    sigmoid(S1, S1[:, :], 1)
                    if not first:
                        split_hi(at, 4)
                    act.wait_ge(g_raw, nm * 2 + 2)
                    sigmoid(S2, S2[:, :], 2)
                    if first:
                        yc_round(m0, PAIRS - 1, 1)
                    split_hi(at, 5)
                    split_hi(at, 6)
                    act.wait_ge(merged, nm + 2)
                    af(mid_hi[:, bass.ds(m, 1), :].rearrange("p a t -> p (a t)"), N0[:, :], ACT.Copy).then_inc(mid_hi_ok, 1)

                merge(0, True)
                with act.Fori(1, KD) as m:
                    merge(m, False)

                with act.Fori(0, 2) as i:
                    for c in range(4):
                        split_hi(pl["O"](i), c + 3)
                        xg_round(l * (2 * KD) + (i * 4 + (KD + c + 1)), bass.ds(i * 4 + c, 1),
                                 par[:, bass.ds(i * 4 + (R_GF + c), 1)])

                def gate_up(p, i, first=False):
                    at = pl["GU"](p, i)
                    f0 = PARTS[p][0]
                    for c in range(4):
                        f = i * 2 + c // 2
                        nf = l * KF + f0 + f
                        if not (first and c == 1):
                            split_hi(at, c + 3)
                        if first and c == 0:
                            split_hi(at, 4)
                            ln_exp_table()
                            act.wait_ge(sq_done, l * 2 + 2)
                            rms_chain(l * CHAINS + (CHAINS - 1), bank_sq, D)
                        if c % 2 == 0:
                            act.wait_ge(silu_in, nf + 1)
                            af(S0[:, :], S0[:, :], ACT.Silu).then_inc(silu_ok, 1)
                        else:
                            act.wait_ge(act_pre, nf + 1)
                            af(mid_hi[:, bass.ds(f, 1), :].rearrange("p a t -> p (a t)"), N0[:, :], ACT.Copy
                               ).then_inc(mid_hi_ok, 1)

                for p, (f0, n) in enumerate(PARTS):
                    if p == 0:
                        gate_up(0, 0, True)
                    with act.Fori(1 if p == 0 else 0, n // 2) as i:
                        gate_up(p, i)
                    with act.Fori(0, 2) as i:
                        for c in range(4):
                            split_hi(pl["WD"](p, i), c + 3)
                            if p == len(PARTS) - 1:
                                xg_round(l * (2 * KD) + (i * 4 + (2 * KD + c + 1)), bass.ds(i * 4 + c, 1),
                                         par[:, bass.ds(i * 4 + (R_GM + c), 1)])

            for n in range(NT):
                act.wait_ge(o_turned, 2 * n + 1)
                af(toks[:, n, 0:T], bank[(2 * n) % NB][:, :], ACT.Copy).then_inc(o_act, 1)

        @block.vector
        def _(dve):
            tt, ts, stt = nc.vector.tensor_tensor, nc.vector.tensor_scalar, nc.vector.scalar_tensor_tensor
            copy = nc.vector.tensor_copy

            def split_lo(at, c, kc=KD):
                dve.wait_ge(hi_done, at.count(c))
                r, h, w = raw[at.slot(c)], w_hi[at.slot(c)], w_lo[at.slot(c)]
                tt(w[:, 0:kc, :], r[:, 0:kc, :], h[:, 0:kc, :].bitcast(F32), ALU.subtract).then_inc(lo_done, 1)

            def scaled(at, c, dst):
                dve.wait_ge(unit_done, at.count(c, RAW))
                return tt(dst, bank[at.slot(c)][:, :], rstd[:, :], ALU.mult).then_inc(bank_free[at.slot(c)], 1)

            def newton(nth, dst):
                dve.wait_ge(chain, nth + 1)
                stt(N2, N0[:, :], -0.5, N2, ALU.mult, ALU.mult)
                dve.drain()
                stt(dst, N2, 1.5, N1[:, :], ALU.add, ALU.mult).then_inc(chain_done, 1)
                dve.drain()

            def xg_rest(n_hi, c, gain):
                dve.wait_ge(xg_hi_ok, n_hi)
                stt(xg_lo[:, c, :], xT[:, c, :], gain, xg_hi[:, c, :].bitcast(F32), ALU.mult, ALU.subtract
                    ).then_inc(xg_ok, 1)

            def softplus_sum(h3):
                for g, (a, n) in enumerate(S_COLS):
                    dve.wait_ge(z_ln, h3 + (g + 1))
                    stt(t_s[:, a:a + n], z[g][:, 0:n], 0.0, t_s[:, a:a + n], ALU.max, ALU.add).then_inc(sp_ok, 1)

            def softplus_lo(h3):
                for g, (a, n) in enumerate(S_COLS):
                    dve.wait_ge(sp_hi, h3 + (g + 1))
                    tt(s_lo[:, a:a + n], t_s[:, a:a + n], s_hi[:, a:a + n].bitcast(F32), ALU.subtract).then_inc(sp_lo, 1)

            def attention_lo(h3):
                for g, (a, n) in enumerate(S_COLS):
                    dve.wait_ge(a_hi, h3 + (g + 1))
                    tt(s_lo[:, a:a + n], t_s[:, a:a + n], s_hi[:, a:a + n].bitcast(F32), ALU.subtract).then_inc(a_lo, 1)

            def yc_rest(nth, j, e):
                rows = slice(HD * e, HD * e + HD)
                dve.wait_ge(yc_hi_ok, nth + 1)
                flat = lambda t: t[rows, bass.ds(j, 1), :].rearrange("p a t -> p (a t)")
                tt(flat(yc_lo), misc[rows, :], flat(yc_hi).bitcast(F32), ALU.subtract).then_inc(yc_ok, 1)
                dve.drain()
                dve.sem_inc(misc_free, 1)

            def head_norm(nth_chain, s, gain):
                newton(nth_chain, N1[:, :])
                stt(s[:, :], s[:, :], gain, N1[:, :], ALU.mult, ALU.mult).then_inc(qk_nrm, 1)

            def head_rest(s, hi, lo, n_qk):
                dve.wait_ge(qk_hi, n_qk)
                tt(lo[:, :], s[:, :], hi[:, :].bitcast(F32), ALU.subtract).then_inc(qk_ok, 1)

            dve.sem_inc(unit_done, RAW)
            dve.sem_inc(a_exp, 3)
            dve.sem_inc(merged, 1)
            for s in (chain_done, misc_free, yb_bank_free):
                dve.sem_inc(s, 1)
            nc.vector.memset(eps[:, :], EPS)
            nc.vector.memset(conv_in[:, 0:2], 0.0)
            nc.vector.memset(head_ones[:, :], 0.0)
            nc.vector.memset(N0[:, 0:P], -1.0)
            dve.drain()
            nc.vector.memset(head_ones[0:HD, 0:HD], 1.0)
            nc.vector.memset(head_ones[HD:P, HD:P], 1.0)
            dve.wait_ge(ident_ok, 1)
            copy(ident_r[:, :], ident[:, :])
            copy(neg_tri[:, :], S0[:, 0:P])
            copy(mask_add[:, :], S1[:, 0:P])
            copy(neg_ones[:, :], N0[:, 0:P])
            dve.drain()
            dve.sem_inc(consts, 1)

            dve.wait_ge(misc_done, 1)
            copy(gain0[:, :], misc[:, 0:KD]).then_inc(par_ok, 1)
            dve.drain()
            dve.sem_inc(misc_free, 1)
            for c in range(KD):
                dve.wait_ge(x_turned, c + 1)
                copy(xT[:, c, :], bank[c % NB][:, :]).then_inc(x_new, 1)
                if c >= 1:
                    xg_rest(c, c - 1, gain0[:, c - 1:c])
            xg_rest(KD, KD - 1, gain0[:, KD - 1:KD])
            for b in range(NB):
                dve.sem_inc(bank_free[b], 1)
            start = Units(0)
            for c in range(AHEAD):
                split_lo(start, c)

            with dve.Fori(0, L) as l:
                pl = places(l)
                m0 = l * M_LAYER + 1
                at = pl["P"]
                nchain = l * CHAINS
                def layer_norm(n):
                    e = (S0, S1)[n % 2]
                    if n >= 2:
                        dve.drain()
                    ts(e[:, :], v_tok[:, n, :], ln_mv[:, n, 0:1], ln_rstd[:, n:n + 1], ALU.subtract, ALU.mult)
                    dve.drain()
                    tt(e[:, :], e[:, :], ln_g[:, :], ALU.mult)
                    dve.drain()
                    tt(e[:, :], e[:, :], ln_b[:, :], ALU.add).then_inc(ln_pre, 1)

                def layer_norm_lo(n):
                    dve.wait_ge(ln_hi, l * 4 + n + 1)
                    tt(yb_lo[:, :, n * P:(n + 1) * P], (S0, S1)[n % 2][:, :].rearrange("p (g c) -> p g c", g=KC),
                       yb_hi[:, :, n * P:(n + 1) * P].bitcast(F32), ALU.subtract).then_inc(ln_ok, 1)

                def keep_tokens(c, src):
                    return copy(v_tok[:, :, c * P:(c + 1) * P], src[:, :].rearrange("p (n c) -> p n c", n=NT))

                split_lo(at, 3)
                split_lo(at, 4)
                newton(nchain, rstd[:, :])
                for c in range(4):
                    scaled(at, c, gates[:, c, :])
                    dve.drain()
                    dve.sem_inc(sv_raw, 1)
                    if c >= 2:
                        split_lo(at, c + 3)
                dve.wait_ge(misc_done, m0 + 1)
                copy(par[:, 0:NPAR], misc[:, 0:NPAR])
                dve.drain()
                ts(par[:, R_GQ:R_GQ + 1], par[:, R_GQ:R_GQ + 1], HD ** -0.5, None, ALU.mult)
                dve.drain()
                dve.sem_inc(par_ok, 1)
                dve.sem_inc(misc_free, 1)
                scaled(at, 4, QT[:, :])
                dve.drain()
                dve.sem_inc(qk_raw, 1)
                split_lo(at, 7)
                for c in range(3):
                    dve.wait_ge(sv_turned, l * 3 + c + 1)
                    keep_tokens(c, sv_bank[c])
                scaled(at, 5, KT[:, :])
                dve.drain()
                dve.sem_inc(qk_raw, 1)
                dve.wait_ge(misc_done, m0 + 2)
                keep_tokens(3, misc)
                dve.drain()
                dve.sem_inc(misc_free, 1)
                for n in range(NT):
                    nc.vector.bn_stats(ln_stats[:, n, :], v_tok[:, n, :])
                dve.drain()
                for n in range(NT):
                    nc.vector.bn_aggr(ln_mv[:, n, :], ln_stats[:, n, :])
                dve.drain()
                dve.sem_inc(ln_var, 1)
                split_lo(at, 8)
                scaled(at, 6, gates[:, 4, :])
                dve.wait_ge(ln_chain, l + 1)
                stt(ln_t[:, :], ln_v[:, :], -0.5, ln_t[:, :], ALU.mult, ALU.mult)
                dve.drain()
                stt(ln_rstd[:, :], ln_t[:, :], 1.5, ln_r[:, :], ALU.add, ALU.mult)
                dve.drain()
                head_norm(nchain + 1, QT, par[:, R_GQ:R_GQ + 1])
                split_lo(at, 9)
                dve.wait_ge(ln_in, l * 48 + 48)
                layer_norm(0)
                head_rest(QT, q_hi, q_lo, l * 8 + 1)
                scaled(at, 7, gates[:, 5, :])
                head_norm(nchain + 2, KT, par[:, R_GK:R_GK + 1])
                layer_norm(1)
                layer_norm_lo(0)
                split_lo(at, 10)
                scaled(at, 8, gates[:, 6, :])
                head_rest(KT, k_hi, k_lo, l * 8 + 2)
                layer_norm(2)
                layer_norm_lo(1)
                split_lo(at, 11)
                layer_norm(3)
                dve.wait_ge(sw_hi_ok, l + 1)
                tt(sw_lo[:, :, :], misc[:, :].rearrange("p (g t) -> p g t", g=KC), sw_hi[:, :, :].bitcast(F32),
                   ALU.subtract)
                dve.drain()
                dve.sem_inc(misc_free, 1)
                scaled(at, 9, gates[:, 7, :])
                layer_norm_lo(2)
                layer_norm_lo(3)
                split_lo(at, 12)
                m0 = m0 + M_P

                def pair(j, last, m0):
                    at = pl["A"](j)
                    h3 = l * 24 + j * 6
                    pairs = l * PAIRS + j
                    j1 = bass.ds(j, 1)

                    def flat(t):
                        return t[:, j1, :].rearrange("p a t -> p (a t)")

                    def tap(k):
                        return par[:, bass.ds(j + (R_CW + 4 * k), 1)]

                    def convolution():
                        dve.drain()
                        tt(conv_in[:, 2:2 + T], S1[:, :], S2[:, :], ALU.mult)
                        dve.drain()
                        ts(S1[:, :], conv_in[:, 2:2 + T], tap(2), par[:, bass.ds(j + R_CB, 1)], ALU.mult, ALU.add)
                        dve.drain()
                        stt(S1[:, :], conv_in[:, 1:1 + T], tap(1), S1[:, :], ALU.mult, ALU.add)
                        dve.drain()
                        stt(S1[:, :], conv_in[:, 0:T], tap(0), S1[:, :], ALU.mult, ALU.add)
                        dve.drain()
                        tt(S1[:, :], S1[:, :], S0[:, :], ALU.mult).then_inc(ya_pre, 1)

                    def ya_rest():
                        dve.wait_ge(ya_hi_ok, pairs + 1)
                        tt(flat(ya_lo), S1[:, :], flat(ya_hi).bitcast(F32), ALU.subtract).then_inc(ya_ok, 1)

                    def yb_rest():
                        dve.wait_ge(yb_hi_ok, pairs + 1)
                        tt(flat(yb_lo), N0[:, :], flat(yb_hi).bitcast(F32), ALU.subtract).then_inc(yb_ok, 1)

                    def v_rest():
                        dve.wait_ge(v_hi_ok, pairs + 1)
                        tt(v_lo[:, :, :], misc[:, :].rearrange("p (n c) -> p n c", n=NT), v_hi[:, :, :].bitcast(F32),
                           ALU.subtract).then_inc(v_ok, 1)
                        dve.drain()
                        dve.sem_inc(misc_free, 1)

                    softplus_sum(h3)
                    softplus_lo(h3)
                    scaled(at, 0, N0[:, :])
                    dve.drain()
                    dve.sem_inc(v_raw, 1)
                    split_lo(at, 3)
                    if last:
                        scaled(at, 1, S0[:, :])
                        split_lo(at, 4)
                        v_rest()
                        scaled(at, 2, S1[:, :])
                        split_lo(at, 5)
                        attention_lo(h3)
                        scaled(at, 3, S2[:, :])
                        split_lo(at, 6)
                        yc_rest(l * 8 + j * 2, j, 0)
                        softplus_sum(h3 + 3)
                        convolution()
                        softplus_lo(h3 + 3)
                        scaled(at, 4, S2[:, :])
                        dve.drain()
                        dve.sem_inc(u_raw, 1)
                        ya_rest()
                        split_lo(at, 7)
                        mixed(m0 + 2, j1)
                        scaled(at, 5, flat(gates))
                        with_u(pairs)
                        split_lo(at, 8)
                        yb_rest()
                        return
                    scaled(at, 1, QT[:, :])
                    dve.drain()
                    dve.sem_inc(qk_raw, 1)
                    split_lo(at, 4)
                    v_rest()
                    scaled(at, 2, KT[:, :])
                    dve.drain()
                    dve.sem_inc(qk_raw, 1)
                    split_lo(at, 5)
                    attention_lo(h3)
                    nch = l * CHAINS + (j * 2 + 3)
                    head_norm(nch, QT, par[:, R_GQ:R_GQ + 1])
                    scaled(at, 3, S0[:, :])
                    split_lo(at, 6)
                    yc_rest(l * 8 + j * 2, j, 0)
                    softplus_sum(h3 + 3)
                    head_rest(QT, q_hi, q_lo, l * 8 + (j * 2 + 3))
                    scaled(at, 4, S1[:, :])
                    split_lo(at, 7)
                    softplus_lo(h3 + 3)
                    head_norm(nch + 1, KT, par[:, R_GK:R_GK + 1])
                    scaled(at, 5, S2[:, :])
                    split_lo(at, 8)
                    mixed(m0 + 4, j1)
                    head_rest(KT, k_hi, k_lo, l * 8 + (j * 2 + 4))
                    convolution()
                    scaled(at, 6, S2[:, :])
                    dve.drain()
                    dve.sem_inc(u_raw, 1)
                    ya_rest()
                    split_lo(at, 9)
                    attention_lo(h3 + 3)
                    scaled(at, 7, flat(gates))
                    with_u(pairs)
                    split_lo(at, 10)
                    yb_rest()
                    yc_rest(l * 8 + (j * 2 + 1), j, 1)

                def mixed(n_misc, j1):
                    dve.wait_ge(misc_done, n_misc + 1)
                    b = sgu_bias[:, j1, :].broadcast_to([P, NT, P])
                    tt(N0[:, :].rearrange("p (n t) -> p n t", n=NT), misc[:, :].rearrange("p (n t) -> p n t", n=NT),
                       b, ALU.add).then_inc(misc_free, 1)

                def with_u(pairs):
                    dve.drain()
                    dve.wait_ge(u_ok, pairs + 1)
                    tt(N0[:, :], N0[:, :], S2[:, :], ALU.mult).then_inc(yb_pre, 1)

                with dve.Fori(0, PAIRS - 1) as j:
                    pair(j, False, m0 + j * M_PAIR)
                m0 = m0 + (PAIRS - 1) * M_PAIR
                pair(PAIRS - 1, True, m0)
                m0 = m0 + M_PAIR_LAST

                def merge(m, first):
                    at = pl["M"](m)
                    nm = l * KD + m
                    m1 = bass.ds(m, 1)
                    scaled(at, 0, S1[:, :])
                    dve.drain()
                    dve.sem_inc(g_raw, 1)
                    split_lo(at, 3, KC)
                    if first:
                        split_lo(at, 4)
                        attention_lo(l * 24 + 21)
                    scaled(at, 1, S2[:, :])
                    dve.drain()
                    dve.sem_inc(g_raw, 1)
                    if first:
                        yc_rest(l * 8 + 7, PAIRS - 1, 1)
                    else:
                        split_lo(at, 4)
                    dve.wait_ge(g_sig, nm * 3 + 2)
                    dve.wait_ge(unit_done, at.count(2, RAW))
                    tt(N0[:, :], bank[at.slot(2)][:, :], S0[:, :], ALU.mult).then_inc(bank_free[at.slot(2)], 1)
                    tt(N1[:, :], bank_yb[:, :], S1[:, :], ALU.mult).then_inc(yb_bank_free, 1)
                    dve.drain()
                    tt(N0[:, :], N0[:, :], N1[:, :], ALU.add)
                    split_lo(at, 5)
                    dve.drain()
                    dve.wait_ge(g_sig, nm * 3 + 3)
                    dve.wait_ge(unit_done, at.count(3, RAW))
                    tt(N1[:, :], bank[at.slot(3)][:, :], S2[:, :], ALU.mult).then_inc(bank_free[at.slot(3)], 1)
                    dve.drain()
                    tt(N0[:, :], N0[:, :], N1[:, :], ALU.add).then_inc(merged, 1)
                    dve.wait_ge(mid_hi_ok, l * (KD + KF) + m + 1)
                    tt(mid_lo[:, m1, :].rearrange("p a t -> p (a t)"), N0[:, :],
                       mid_hi[:, m1, :].rearrange("p a t -> p (a t)").bitcast(F32), ALU.subtract).then_inc(mid_ok, 1)
                    split_lo(at, 6)

                merge(0, True)
                with dve.Fori(1, KD) as m:
                    merge(m, False)

                def renew(at, c, i, prep, gain_row=0, news=0):
                    dve.wait_ge(unit_done, at.count(c, RAW))
                    xc = bass.ds(i * 4 + c, 1)
                    xs = xT[:, xc, :].rearrange("p a t -> p (a t)")
                    tt(xs, xs, bank[at.slot(c)][:, :], ALU.add).then_inc(bank_free[at.slot(c)], 1)
                    if prep:
                        dve.drain()
                        dve.sem_inc(x_new, 1)
                        dve.wait_ge(xg_hi_ok, news + (i * 4 + (c + 1)))
                        stt(xg_lo[:, xc, :].rearrange("p a t -> p (a t)"), xs, par[:, bass.ds(i * 4 + (gain_row + c), 1)],
                            xg_hi[:, xc, :].rearrange("p a t -> p (a t)").bitcast(F32), ALU.mult, ALU.subtract
                            ).then_inc(xg_ok, 1)

                with dve.Fori(0, 2) as i:
                    at = pl["O"](i)
                    for c in range(4):
                        renew(at, c, i, True, R_GF, l * (2 * KD) + KD)
                        split_lo(at, c + 3)

                def gate_up(p, i, first=False):
                    at = pl["GU"](p, i)
                    f0 = PARTS[p][0]
                    for c in range(4):
                        f = i * 2 + c // 2
                        nf = l * KF + f0 + f
                        f1 = bass.ds(f, 1)
                        if first and c == 0:
                            split_lo(at, 3)
                            split_lo(at, 4)
                            newton(l * CHAINS + (CHAINS - 1), rstd[:, :])
                        if c % 2 == 0:
                            scaled(at, c, S0[:, :])
                            dve.drain()
                            dve.sem_inc(silu_in, 1)
                        else:
                            scaled(at, c, S1[:, :])
                            dve.drain()
                            dve.wait_ge(silu_ok, nf + 1)
                            tt(N0[:, :], S0[:, :], S1[:, :], ALU.mult).then_inc(act_pre, 1)
                            dve.wait_ge(mid_hi_ok, l * (KD + KF) + (KD + f0) + f + 1)
                            tt(mid_lo[:, f1, :].rearrange("p a t -> p (a t)"), N0[:, :],
                               mid_hi[:, f1, :].rearrange("p a t -> p (a t)").bitcast(F32), ALU.subtract
                               ).then_inc(mid_ok, 1)
                        if not (first and c <= 1):
                            split_lo(at, c + 3)

                for p, (f0, n) in enumerate(PARTS):
                    if p == 0:
                        gate_up(0, 0, True)
                    with dve.Fori(1 if p == 0 else 0, n // 2) as i:
                        gate_up(p, i)
                    with dve.Fori(0, 2) as i:
                        at = pl["WD"](p, i)
                        for c in range(4):
                            renew(at, c, i, p == len(PARTS) - 1, R_GM, l * (2 * KD) + 2 * KD)
                            split_lo(at, c + 3)

            for n in range(NT):
                dve.wait_ge(o_turned, 2 * n + 2)
                copy(toks[:, n, T:2 * T], bank[(2 * n + 1) % NB][:, :]).then_inc(o_dve, 1)


def kernel(**inputs):
    import numpy as np
    import concourse.bacc as bacc
    from concourse.bass_utils import run_bass_kernel_spmd

    names = ["x", "mix_norm_g", "w_in", "b_gate", "conv_w", "conv_b", "sgu_ln_g", "sgu_ln_b", "sgu_w", "sgu_b",
             "q_norm_g", "k_norm_g", "w_branch_out", "w_o", "ffn_norm_g", "w_gate_up", "w_down"]
    nc = bacc.Bacc("TRN2", target_bir_lowering=False, num_devices=1)
    arrays, args = {}, []
    for name in names:
        a = np.ascontiguousarray(inputs[name])
        arrays[f"in_{name}"] = a
        args.append(nc.dram_tensor(f"in_{name}", a.shape, mybir.dt.from_np(a.dtype), kind="ExternalInput").ap())
    out = nc.dram_tensor("out_x", (1, T, D), F32, kind="ExternalOutput").ap()
    build(nc, *args, out)
    got = run_bass_kernel_spmd(nc, [arrays], core_ids=[0])
    return got.results[0]["out_x"]
```

```python
from contextlib import ExitStack

import concourse.bass as bass
from concourse import mybir

P = 128
T = 512
NT = T // P
D = 1024
KD = D // P
L = 2
CH = D // 2
KC = CH // P
HD = 64
PAIRS = CH // (2 * HD)
DFF = 2816
KF = DFF // P
PARTS = [(0, 8), (8, 8), (16, 6)]
EPS = 1e-6
MASKED = -1e30

C_B, C_C, C_X, C_U, C_SV, C_Q, C_K, C_V, C_G = [CH * i for i in range(8)] + [8 * CH]

RAW = 4
AHEAD = 3
NB = 4

UP, UA, UM, UO = 10, 8 * 3 + 6, 4 * KD, KD
UF = [2 * n + KD for _, n in PARTS]
B_P, B_A, B_M, B_O = 0, UP, UP + UA, UP + UA + UM
B_F = [B_O + UO, B_O + UO + UF[0], B_O + UO + UF[0] + UF[1]]
UL = B_F[2] + UF[2]
assert UL % RAW == 0

R_GM, R_GF, R_BG, R_CW, R_CB, R_GQ, R_GK, NPAR = 0, 8, 16, 40, 52, 56, 57, 58

Z_BLOCKS = [(0, [0]), (1, [1, 3]), (2, [2])]
Z_AT = {0: 0, 1: 0, 3: 384, 2: 0}
S_AT = {0: 0, 1: 512, 3: 896, 2: 1024}
S_COLS = [(0, 512), (512, 512), (1024, 256)]

M_P, M_PAIR, M_PAIR_LAST = 5, 6, 3
M_LAYER = M_P + (PAIRS - 1) * M_PAIR + M_PAIR_LAST + 1
CHAINS = 2 + 2 * PAIRS

F32 = mybir.dt.float32
F32R = mybir.dt.float32r
ALU = mybir.AluOpType
ACT = mybir.ActivationFunctionType


class Units:

    def __init__(self, quad, off=0):
        self.quad, self.off = quad, off

    def count(self, c, credit=0):
        return self.quad * 4 + (self.off + c + 1 + credit)

    def round(self, c, step=1):
        return self.quad * step + ((self.off + c) // 4 + 1) * step

    def slot(self, c):
        return (self.off + c) % 4


def places(l):
    q = UL // 4
    return {
        "P": Units(l * q),
        "A": lambda j: Units(l * q + (B_A // 4) + j * 2, B_A % 4),
        "M": lambda m: Units(l * q + B_M // 4 + m),
        "O": lambda i: Units(l * q + B_O // 4 + i),
        "GU": lambda p, i: Units(l * q + B_F[p] // 4 + i),
        "WD": lambda p, i: Units(l * q + (B_F[p] + 2 * PARTS[p][1]) // 4 + i),
    }


def build(nc, x, mix_norm_g, w_in, b_gate, conv_w, conv_b, sgu_ln_g, sgu_ln_b, sgu_w, sgu_b,
          q_norm_g, k_norm_g, w_branch_out, w_o, ffn_norm_g, w_gate_up, w_down, out):
    ctx = ExitStack()
    with ctx:
        plan = [(nc.sbuf_base + 31) // 32 * 32]

        def sb(name, shape, dt=F32, at=None):
            size = 4
            for n in shape[1:]:
                size *= n
            if at is None:
                at = plan[0]
                plan[0] += (size + 31) // 32 * 32
            t = nc.alloc_sbuf_tensor_at(name, shape, dt, offset=at)
            offsets[name] = at
            return t

        offsets = {}

        def sem(name):
            return ctx.enter_context(nc.semaphore(name))

        xT = sb("xT", [P, KD, T])
        xg_hi = sb("xg_hi", [P, KD, T], F32R)
        xg_lo = sb("xg_lo", [P, KD, T], F32R)
        raw = [sb(f"raw{i}", [P, KD, P]) for i in range(RAW)]
        w_lo = [sb(f"w_lo{i}", [P, KD, P], F32R, at=offsets[f"raw{i}"]) for i in range(RAW)]
        w_hi = [sb(f"w_hi{i}", [P, KD, P], F32R) for i in range(RAW)]
        ident = sb("ident", [P, P])
        head_ones = sb("head_ones", [P, P], F32R)
        ident_r = sb("ident_r", [P, P], F32R)
        neg_tri = sb("neg_tri", [P, P], F32R)
        neg_ones = sb("neg_ones", [P, P], F32R)
        mask_add = sb("mask_add", [P, P], F32R)
        rstd = sb("rstd", [P, T])
        sgu_bias = sb("sgu_bias", [P, KC, P])
        sw_hi = sb("sw_hi", [P, KC, P], F32R)
        sw_lo = sb("sw_lo", [P, KC, P], F32R)
        eps = sb("eps", [P, 1])
        par = sb("par", [P, 64])
        gain0 = sb("gain0", [P, KD])
        ln_stats = sb("ln_stats", [P, NT, 6])
        ln_mv = sb("ln_mv", [P, NT, 2])
        ln_v = sb("ln_v", [P, NT])
        ln_r = sb("ln_r", [P, NT])
        ln_t = sb("ln_t", [P, NT])
        ln_rstd = sb("ln_rstd", [P, NT])
        ya_hi = sb("ya_hi", [P, KC, T], F32R)
        ya_lo = sb("ya_lo", [P, KC, T], F32R)
        yb_hi = sb("yb_hi", [P, KC, T], F32R)
        yb_lo = sb("yb_lo", [P, KC, T], F32R)
        yc_hi = sb("yc_hi", [P, KC, T], F32R)
        yc_lo = sb("yc_lo", [P, KC, T], F32R)
        v_tok = sb("v_tok", [P, NT, CH], at=offsets["yc_hi"])
        ln_g = sb("ln_g", [P, CH], at=offsets["yc_lo"])
        ln_b = sb("ln_b", [P, CH], at=offsets["yc_lo"] + 4 * CH)
        sw_raw = sb("sw_raw", [P, KC, P], at=offsets["yc_lo"] + 8 * CH)
        par_rows = sb("par_rows", [64, P], at=offsets["yc_lo"] + 8 * CH + 4 * KC * P)
        gates = sb("gates", [P, KD, T])
        toks = gates[:, :, :].rearrange("p a b -> p (a b)").rearrange("p (n d) -> p n d", n=NT)
        suf_hi = sb("suf_hi", [P, 2 * P], F32R, at=offsets["gates"] + 3 * 4 * T)
        suf_lo = sb("suf_lo", [P, 2 * P], F32R, at=offsets["gates"] + 3 * 4 * T + 8 * P)
        suf = sb("suf", [P, 2 * P], at=offsets["suf_lo"])
        S0 = sb("S0", [P, T])
        S1 = sb("S1", [P, T])
        S2 = sb("S2", [P, T])
        sq_hi = sb("sq_hi", [P, T], F32R)
        sq_lo = sb("sq_lo", [P, T], F32R, at=offsets["S2"])
        QT = sb("QT", [P, T])
        KT = sb("KT", [P, T])
        conv_in = sb("conv_in", [P, 2 + T])
        N0 = sb("N0", [P, T])
        N1 = sb("N1", [P, T])
        N2 = conv_in[:, 2:2 + T]
        sq_sum, sq_one = S2[:, :], N1[:, :]
        over = plan[0]
        q_twice = sb("q_twice", [P, 2, T], F32R)
        k_both = sb("k_both", [P, 2, T], F32R)
        q_lo = sb("q_lo", [P, T], F32R)
        v_both = sb("v_both", [P, NT * 2, 2, HD], F32R)
        mix_hi = sb("mix_hi", [P, NT, P], F32R)
        mix_lo = sb("mix_lo", [P, NT, P], F32R)
        t_s = sb("t_s", [P, 1280])
        s_hi = sb("s_hi", [P, 1280], F32R)
        s_lo = sb("s_lo", [P, 1280], F32R)
        mid_hi = sb("mid_hi", [P, 8, T], F32R, at=over)
        mid_lo = sb("mid_lo", [P, 8, T], F32R, at=over + 8 * 4 * T)
        plan[0] = max(plan[0], over + 16 * 4 * T)
        assert plan[0] <= nc.sbuf_usable_end, plan[0]

        bank = [ctx.enter_context(nc.psum_tensor(f"bank{i}", [P, T], F32)) for i in range(NB)]
        z = [ctx.enter_context(nc.psum_tensor(f"z{i}", [P, T], F32)) for i in range(3)]
        misc = ctx.enter_context(nc.psum_tensor("misc", [P, T], F32))
        bank_yb, bank_sq = z[0], z[1]
        sv_bank = [z[0], z[2], z[1]]
        out_bank = [[*z, misc], bank]

        raw_full = [sem(f"raw_full{i}") for i in range(RAW)]
        hi_done = sem("hi_done")
        lo_done = sem("lo_done")
        unit_done = sem("unit_done")
        bank_free = [sem(f"bank_free{i}") for i in range(NB)]
        passed = sem("passed")
        consts = sem("consts")
        ident_ok = sem("ident_ok")
        gain_in = sem("gain_in")
        x_in = [sem(f"x_in{i}") for i in range(4)]
        par_in = sem("par_in")
        ln_in = sem("ln_in")
        sw_in = sem("sw_in")
        sw_masked = sem("sw_masked")
        par_ok = sem("par_ok")
        x_turned = sem("x_turned")
        x_new = sem("x_new")
        xg_hi_ok = sem("xg_hi_ok")
        xg_ok = sem("xg_ok")
        sq_ok = sem("sq_ok")
        sq_done = sem("sq_done")
        chain = sem("chain")
        chain_done = sem("chain_done")
        misc_done = sem("misc_done")
        misc_free = sem("misc_free")
        sv_raw = sem("sv_raw")
        sv_ok = sem("sv_ok")
        sv_turned = sem("sv_turned")
        sv_kept = sem("sv_kept")
        ln_var = sem("ln_var")
        ln_chain = sem("ln_chain")
        ln_pre = sem("ln_pre")
        ln_hi = sem("ln_hi")
        ln_ok = sem("ln_ok")
        sw_hi_ok = sem("sw_hi_ok")
        qk_raw = sem("qk_raw")
        qk_sq = sem("qk_sq")
        qk_nrm = sem("qk_nrm")
        qk_hi = sem("qk_hi")
        q_ok = sem("q_ok")
        k_ok = sem("k_ok")
        v_raw = sem("v_raw")
        v_hi_ok = sem("v_hi_ok")
        v_ok = sem("v_ok")
        slab_in = sem("slab_in")
        z_done = sem("z_done")
        z_ln = sem("z_ln")
        sp_ok = sem("sp_ok")
        sp_hi = sem("sp_hi")
        sp_lo = sem("sp_lo")
        suf_ok = sem("suf_ok")
        cum_done = sem("cum_done")
        a_exp = sem("a_exp")
        a_hi = sem("a_hi")
        a_lo = sem("a_lo")
        yc_half_ok = sem("yc_half_ok")
        yc_sum = sem("yc_sum")
        yc_hi_ok = sem("yc_hi_ok")
        yc_ok = sem("yc_ok")
        ya_pre = sem("ya_pre")
        ya_hi_ok = sem("ya_hi_ok")
        ya_ok = sem("ya_ok")
        u_raw = sem("u_raw")
        u_ok = sem("u_ok")
        yb_pre = sem("yb_pre")
        yb_hi_ok = sem("yb_hi_ok")
        yb_ok = sem("yb_ok")
        g_raw = sem("g_raw")
        g_sig = sem("g_sig")
        merged = sem("merged")
        yb_bank_free = sem("yb_bank_free")
        silu_in = sem("silu_in")
        silu_ok = sem("silu_ok")
        act_pre = sem("act_pre")
        mid_hi_ok = sem("mid_hi_ok")
        mid_ok = sem("mid_ok")
        o_turned0 = sem("o_turned0")
        o_turned1 = sem("o_turned1")
        o_act = sem("o_act")
        o_dve = sem("o_dve")
        stored = sem("stored")

        block = ctx.enter_context(nc.Block())

        @block.sync
        def _(sp):
            def cols(w, l, c0, r0=0, kc=KD):
                return w[l].rearrange("(c p) n -> p c n", p=P)[:, r0:r0 + kc, bass.ds(c0, P)]

            def load(at, c, src, kc=KD):
                sp.wait_ge(unit_done, at.count(c))
                sp.dma_start(raw[at.slot(c)][:, 0:kc, :], src).then_inc(raw_full[at.slot(c)], 16)

            sp.dma_start(par_rows[0:KD, :], mix_norm_g[0].rearrange("(a p) -> a p", p=P)).then_inc(gain_in, 16)
            x_toks = x.rearrange("b (n p) d -> p (b n) d", p=P)
            for i in range(4):
                cut = slice(i * D // 4, (i + 1) * D // 4)
                sp.dma_start(toks[:, :, cut], x_toks[:, :, cut]).then_inc(x_in[i], 16)

            with sp.Fori(0, L) as l:
                pl = places(l)
                order = [C_SV, C_SV + P, C_SV + 2 * P, C_SV + 3 * P, C_Q, C_K] + [C_G + P * m for m in range(4, 8)]
                for c, c0 in enumerate(order):
                    load(pl["P"], c, cols(w_in, l, c0))
                    if c == 3:
                        sp.wait_ge(par_ok, l + 1)
                        sp.sem_inc(passed, 1)
                        rows = [(mix_norm_g[1 - l], R_GM, 8), (ffn_norm_g[l], R_GF, 8),
                                (b_gate[l], R_BG, 24), (conv_b[l], R_CB, 4)]
                        for src, r, n in rows:
                            sp.dma_start(par_rows[r:r + n, :], src.rearrange("(a p) -> a p", p=P)).then_inc(par_in, 16)
                        sp.dma_start(par_rows[R_CW:R_CW + 12, :],
                                     conv_w[l].rearrange("k (a p) -> (k a) p", p=P)).then_inc(par_in, 16)
                        for src, r in ((q_norm_g, R_GQ), (k_norm_g, R_GK)):
                            for h in range(2):
                                sp.dma_start(par_rows[r:r + 1, h * HD:(h + 1) * HD],
                                             src[l].rearrange("(a p) -> a p", a=1)).then_inc(par_in, 16)
                    if c == 4:
                        sp.dma_start(ln_g[:, :], sgu_ln_g[l].partition_broadcast(P)).then_inc(ln_in, 16)
                        sp.dma_start(ln_b[:, :], sgu_ln_b[l].partition_broadcast(P)).then_inc(ln_in, 16)
                        sp.dma_start(sgu_bias[:, :, :].rearrange("p g t -> p (g t)"),
                                     sgu_b[l].rearrange("g t -> (g t)").partition_broadcast(P)).then_inc(ln_in, 16)
                        sp.dma_start(sw_raw[:, :, :], sgu_w[l].rearrange("g t s -> t g s")).then_inc(sw_in, 16)

                def attention_loads(j, last):
                    at = pl["A"](j)
                    order = [C_V + P * j]
                    if not last:
                        order += [C_Q + P * (j + 1), C_K + P * (j + 1)]
                    order += [C_B + P * j, C_C + P * j, C_X + P * j, C_U + P * j, C_G + P * j]
                    for c, c0 in enumerate(order):
                        load(at, c, cols(w_in, l, c0))

                with sp.Fori(0, PAIRS - 1) as j:
                    attention_loads(j, False)
                attention_loads(PAIRS - 1, True)

                with sp.Fori(0, KD) as m:
                    at = pl["M"](m)
                    load(at, 0, cols(w_in, l, m * P + (C_G + D)))
                    load(at, 1, cols(w_in, l, m * P + (C_G + 2 * D)))
                    wb = w_branch_out[l].rearrange("n (c p) d -> p (n c) d", p=P)
                    load(at, 2, wb[:, 0:2 * KC, bass.ds(m * P, P)])
                    load(at, 3, wb[:, 2 * KC:3 * KC, bass.ds(m * P, P)], KC)

                with sp.Fori(0, 2) as i:
                    for c in range(4):
                        load(pl["O"](i), c, cols(w_o, l, i * (4 * P) + c * P))

                for p, (f0, n) in enumerate(PARTS):
                    with sp.Fori(0, n // 2) as i:
                        for c in range(4):
                            load(pl["GU"](p, i), c,
                                 cols(w_gate_up, l, i * (2 * P) + (f0 + c // 2) * P + (c % 2) * DFF))
                    r0 = min(f0, KF - KD)
                    with sp.Fori(0, 2) as i:
                        for c in range(4):
                            load(pl["WD"](p, i), c, cols(w_down, l, i * (4 * P) + c * P, r0))

            end = Units(L * UL // 4)
            for c in range(AHEAD):
                load(end, c, cols(w_o, 0, c * P))
            for half, copied in enumerate((o_act, o_dve)):
                cut = slice(half * T, (half + 1) * T)
                for n in range(NT):
                    sp.wait_ge(copied, n + 1)
                    sp.dma_start(out[0, n * P:(n + 1) * P, cut], toks[:, n, cut]).then_inc(stored, 16)
            sp.wait_ge(stored, 16 * 2 * NT)

        @block.gpsimd
        def _(pool):
            def triangle(t, keep, fill, base, mult, step):
                nc.gpsimd.affine_select(out=t, in_=t, compare_op=keep, fill=fill, base=base,
                                        pattern=[[step, P]], channel_multiplier=mult)

            nc.gpsimd.memset(ident[:, :], 0.0)
            nc.gpsimd.memset(S0[:, 0:P], -1.0)
            nc.gpsimd.memset(S1[:, 0:P], 0.0)
            pool.drain()
            triangle(ident[:, :], ALU.not_equal, 1.0, 0, 1, -1)
            triangle(S0[:, 0:P], ALU.is_ge, 0.0, 0, 1, -1)
            triangle(S1[:, 0:P], ALU.is_gt, MASKED, 0, -1, 1)
            pool.drain()
            pool.sem_inc(ident_ok, 1)

            def square_sum(nth, c):
                pool.wait_ge(x_new, nth + 1)
                dst = sq_sum if c == 0 else sq_one
                nc.gpsimd.tensor_tensor(dst, xT[:, c, :], xT[:, c, :], ALU.mult)
                pool.drain()
                if c:
                    add = nc.gpsimd.tensor_tensor(sq_sum, sq_sum, sq_one, ALU.add)
                    if c == KD - 1:
                        add.then_inc(sq_ok, 1)
                    pool.drain()

            def head_square(nth, src, n_misc=None):
                pool.wait_ge(qk_raw, nth)
                if n_misc is not None:
                    pool.wait_ge(misc_done, n_misc)
                    pool.sem_inc(passed, 1)
                nc.gpsimd.tensor_tensor(S2[:, :], src[:, :], src[:, :], ALU.mult)
                nc.gpsimd.tensor_tensor(sq_hi[:, :], src[:, :], src[:, :], ALU.mult)
                pool.drain()
                nc.gpsimd.tensor_tensor(sq_lo[:, :], S2[:, :], sq_hi[:, :].bitcast(F32), ALU.subtract
                                        ).then_inc(qk_sq, 1)

            def k_rest(n_qk):
                pool.wait_ge(qk_hi, n_qk)
                pool.sem_inc(passed, 1)
                for e in range(2):
                    own, other = slice(HD * e, HD * e + HD), slice(HD * (1 - e), HD * (1 - e) + HD)
                    last = nc.gpsimd.tensor_tensor(k_both[other, e, :], KT[own, :], k_both[own, e, :].bitcast(F32),
                                                   ALU.subtract)
                last.then_inc(k_ok, 1)

            def suffix(h3):
                pool.wait_ge(sp_ok, h3 + 3)
                t2 = S_AT[2]
                pool.sem_inc(passed, 1)
                nc.gpsimd.tensor_copy(suf[:, 0:P], t_s[:, t2:t2 + P])
                nc.gpsimd.tensor_tensor(suf[:, P:2 * P], t_s[:, t2 + P:t2 + 2 * P], t_s[:, S_AT[3]:S_AT[3] + P], ALU.add)
                pool.drain()
                nc.gpsimd.tensor_copy(suf_hi[:, :], suf[:, :])
                pool.drain()
                nc.gpsimd.tensor_tensor(suf_lo[:, :], suf[:, :], suf_hi[:, :].bitcast(F32), ALU.subtract
                                        ).then_inc(suf_ok, 1)
                pool.drain()

            pool.wait_ge(consts, 1)
            for c in range(KD):
                square_sum(c, c)
            with pool.Fori(0, L) as l:
                pool.wait_ge(sw_in, l * 16 + 16)
                pool.sem_inc(passed, 1)
                for g in range(KC):
                    last = nc.gpsimd.affine_select(
                        out=sw_raw[:, g, :], in_=sw_raw[:, g, :], compare_op=ALU.is_ge, fill=0.0,
                        base=0, pattern=[[-1, P]], channel_multiplier=1)
                last.then_inc(sw_masked, 1)
                m0 = l * M_LAYER + 1
                head_square(l * 8 + 1, QT)
                head_square(l * 8 + 2, KT, m0 + 3)
                k_rest(l * 8 + 2)
                with pool.Fori(0, PAIRS - 1) as j:
                    m = m0 + j * M_PAIR + M_P
                    h3 = l * 24 + j * 6
                    suffix(h3)
                    head_square(l * 8 + (j * 2 + 3), QT)
                    head_square(l * 8 + (j * 2 + 4), KT, m + 2)
                    suffix(h3 + 3)
                    k_rest(l * 8 + (j * 2 + 4))
                for e in range(2):
                    suffix(l * 24 + ((PAIRS - 1) * 6 + 3 * e))
                for half in range(2):
                    for c in range(KD):
                        square_sum(l * (2 * KD) + (KD * (half + 1) + c), c)

        @block.tensor
        def _(pe):
            mm = nc.tensor.matmul

            def unit(at, c, his, los, dsts=None, kc=KD, k0=0, ready=None):
                wh, wl = w_hi[at.slot(c)], w_lo[at.slot(c)]
                dsts = dsts or [bank[at.slot(c)]]
                per = kc // len(dsts)

                def w_hi_passes(k):
                    if ready:
                        pe.wait_ge(ready[0], ready[1] + (k + 1))
                    dst = dsts[k // per]
                    mm(dst[:, :], wh[:, k0 + k, :], his[k], start=(k % per == 0), stop=False)
                    mm(dst[:, :], wh[:, k0 + k, :], los[k], start=False, stop=False)

                def w_lo_pass(k):
                    return mm(dsts[k // per][:, :], wl[:, k0 + k, :], his[k], start=False, stop=(k % per == per - 1))

                pe.wait_ge(bank_free[at.slot(c)], at.round(c))
                pe.wait_ge(hi_done, at.count(c))
                late = 1 if ready else 0
                for k in range(kc - late):
                    w_hi_passes(k)
                pe.wait_ge(lo_done, at.count(c))
                for k in range(kc - late):
                    last = w_lo_pass(k)
                if late:
                    w_hi_passes(kc - 1)
                    last = w_lo_pass(kc - 1)
                last.then_inc(unit_done, 1)

            xh = [xg_hi[:, k, :] for k in range(KD)]
            xl = [xg_lo[:, k, :] for k in range(KD)]

            def turn(dst, src):
                for n in range(4):
                    last = nc.tensor.transpose(dst[:, n * P:(n + 1) * P], src(n), ident[:, :])
                return last

            def four_transposes(n_misc, src, what, value):
                pe.wait_ge(what, value)
                pe.wait_ge(misc_free, n_misc + 1)
                turn(misc, src).then_inc(misc_done, 1)

            def scores(h3, j_pairs, e):
                pe.wait_ge(a_exp, h3 + 3)
                pe.wait_ge(q_ok, j_pairs + 1)
                pe.wait_ge(k_ok, j_pairs + 1)
                rows = slice(HD * e, HD * e + HD)
                for g, blocks in Z_BLOCKS:
                    for n, i in enumerate(blocks):
                        dst = z[g][:, Z_AT[i]:Z_AT[i] + T - P * i]
                        ks, qs = slice(P * i, P * i + P), slice(P * i, T)
                        mm(dst, k_both[:, e, ks], q_twice[:, e, qs], start=(n == 0), stop=False, skip_group_check=True)
                        mm(dst, k_both[rows, e, ks], q_lo[rows, qs], start=False, stop=False, skip_group_check=True)
                    first = [Z_AT[i] // P for i in blocks]
                    dst = z[g][:, :].rearrange("p (b q) -> p b q", q=P)[:, first[0]::(first[-1] - first[0]) or NT, :]
                    mm(dst, ident_r[:, :], mask_add[:, :].rearrange("p (a q) -> p a q", a=1).broadcast_to([P, len(first), P]),
                       start=False, stop=True, skip_group_check=True).then_inc(z_done, 1)

            def cumulate(h3, nth):
                pe.wait_ge(sp_lo, h3 + 3)
                pe.wait_ge(suf_ok, nth + 1)
                parts = [(s_hi, suf_hi), (s_lo, suf_lo)]
                for g, blocks in Z_BLOCKS:
                    for i in blocks:
                        for s, u in parts:
                            terms = [(neg_tri, s, S_AT[i], i)]
                            if i == 0:
                                terms.append((neg_ones, s, S_AT[1], 1))
                            if i < 2:
                                terms.append((neg_ones, u, 0, 2))
                            if i == 2:
                                terms.append((neg_ones, s, S_AT[3], 3))
                            for w, src, a, i2 in terms:
                                width = T - P * i2
                                at = Z_AT[i] + P * (i2 - i)
                                last = mm(z[g][:, at:at + width], w[:, :], src[:, a:a + width],
                                          start=False, stop=(s is s_lo and i2 == terms[-1][3]), skip_group_check=True)
                    last.then_inc(cum_done, 1)

            def attend(h3, n_misc, v_count, e):
                pe.wait_ge(a_lo, h3 + 3)
                pe.wait_ge(v_ok, v_count)
                pe.wait_ge(misc_free, n_misc + 1)
                for i in range(NT):
                    width = T - P * i
                    dst = misc[:, P * i:T]
                    a = slice(S_AT[i], S_AT[i] + width)
                    mm(dst, v_both[:, 2 * i + e, :, :].rearrange("p a d -> p (a d)"), s_hi[:, a],
                       start=(i == 0), stop=(i == NT - 1), skip_group_check=True)
                    last = mm(misc[0:HD, P * i:T], v_both[:, 2 * i + e, 0, :], s_lo[:, a],
                              start=False, stop=(i == NT - 1), skip_group_check=True)
                last.then_inc(misc_done, 1)

            def head_squares(n_misc, nth):
                pe.wait_ge(qk_sq, nth)
                pe.wait_ge(misc_free, n_misc + 1)
                mm(misc[:, :], head_ones[:, :], sq_hi[:, :], start=True, stop=False)
                mm(misc[:, :], head_ones[:, :], sq_lo[:, :], start=False, stop=True).then_inc(misc_done, 1)

            def row_squares(nth):
                pe.wait_ge(sq_ok, nth)
                mm(bank_sq[:, :], neg_ones[:, :].bitcast(F32), sq_sum, start=True, stop=True).then_inc(sq_done, 1)

            def mix(n_misc, j, n_slab):
                pe.wait_ge(slab_in, n_slab)
                pe.wait_ge(misc_free, n_misc + 1)
                for n in range(NT):
                    dst = misc[:, n * P:(n + 1) * P]
                    wh = sw_hi[:, bass.ds(j, 1), :].rearrange("p a t -> p (a t)")
                    wl = sw_lo[:, bass.ds(j, 1), :].rearrange("p a t -> p (a t)")
                    mm(dst, mix_hi[:, n, :], wh, start=True, stop=False)
                    mm(dst, mix_hi[:, n, :], wl, start=False, stop=False)
                    last = mm(dst, mix_lo[:, n, :], wh, start=False, stop=True)
                last.then_inc(misc_done, 1)

            pe.wait_ge(gain_in, 16)
            pe.wait_ge(ident_ok, 1)
            nc.tensor.transpose(misc[:, 0:KD], par_rows[0:KD, :], ident[0:KD, 0:KD]).then_inc(misc_done, 1)
            for c in range(KD):
                if c % 2 == 0:
                    pe.wait_ge(x_in[c // 2], 16)
                if c >= NB:
                    pe.wait_ge(xg_ok, c - NB + 1)
                for n in range(NT):
                    last = nc.tensor.transpose(bank[c % NB][:, n * P:(n + 1) * P], toks[:, n, c * P:(c + 1) * P],
                                               ident[:, :])
                last.then_inc(x_turned, 1)
            pe.wait_ge(consts, 1)

            with pe.Fori(0, L) as l:
                pl = places(l)
                m0 = l * M_LAYER + 1

                at = pl["P"]
                unit(at, 0, xh, xl, ready=(xg_ok, l * (2 * KD)))
                unit(at, 1, xh, xl)
                row_squares(l * 2 + 1)
                unit(at, 2, xh, xl)
                pe.wait_ge(par_in, l * (9 * 16) + 9 * 16)
                pe.wait_ge(misc_free, m0 + 1)
                pe.sem_inc(passed, 1)
                nc.tensor.transpose(misc[:, 0:NPAR], par_rows[0:NPAR, :], ident[0:NPAR, 0:NPAR]).then_inc(misc_done, 1)
                unit(at, 3, xh, xl)
                unit(at, 4, xh, xl)
                for c in range(3):
                    pe.wait_ge(sv_ok, l * 4 + c + 1)
                    turn(sv_bank[c], lambda n: gates[:, c, n * P:(n + 1) * P]).then_inc(sv_turned, 1)
                unit(at, 5, xh, xl)
                four_transposes(m0 + 1, lambda n: gates[:, 3, n * P:(n + 1) * P], sv_ok, l * 4 + 4)
                unit(at, 6, xh, xl)
                head_squares(m0 + 2, l * 8 + 1)
                unit(at, 7, xh, xl)
                head_squares(m0 + 3, l * 8 + 2)
                unit(at, 8, xh, xl)
                four_transposes(m0 + 4, lambda n: sw_raw[:, n, :], sw_masked, l + 1)
                unit(at, 9, xh, xl)
                m0 = m0 + M_P

                def pair(j, last, m0):
                    at = pl["A"](j)
                    h3 = l * 24 + j * 6
                    pairs = l * PAIRS + j
                    scores(h3, pairs, 0)
                    unit(at, 0, xh, xl)
                    unit(at, 1, xh, xl)
                    four_transposes(m0, lambda n: N0[:, n * P:(n + 1) * P], v_raw, pairs + 1)
                    unit(at, 2, xh, xl)
                    cumulate(h3, l * 8 + j * 2)
                    if last:
                        unit(at, 3, xh, xl)
                        attend(h3, m0 + 1, pairs + 1, 0)
                        scores(h3 + 3, pairs, 1)
                        unit(at, 4, xh, xl)
                        mix(m0 + 2, j, (pairs + 1) * 32)
                        unit(at, 5, xh, xl)
                        return
                    head_squares(m0 + 1, l * 8 + (j * 2 + 3))
                    unit(at, 3, xh, xl)
                    attend(h3, m0 + 2, pairs + 1, 0)
                    scores(h3 + 3, pairs, 1)
                    unit(at, 4, xh, xl)
                    head_squares(m0 + 3, l * 8 + (j * 2 + 4))
                    unit(at, 5, xh, xl)
                    mix(m0 + 4, j, (pairs + 1) * 32)
                    unit(at, 6, xh, xl)
                    cumulate(h3 + 3, l * 8 + j * 2 + 1)
                    unit(at, 7, xh, xl)
                    attend(h3 + 3, m0 + 5, pairs + 1, 1)

                with pe.Fori(0, PAIRS - 1) as j:
                    pair(j, False, m0 + j * M_PAIR)
                m0 = m0 + (PAIRS - 1) * M_PAIR
                pair(PAIRS - 1, True, m0)
                m0 = m0 + M_PAIR_LAST

                ybranch = [(ya_hi, ya_lo), (yb_hi, yb_lo)]
                abh = [h[:, k, :] for h, _ in ybranch for k in range(KC)]
                abl = [lo[:, k, :] for _, lo in ybranch for k in range(KC)]
                ch = [yc_hi[:, k, :] for k in range(KC)]
                cl = [yc_lo[:, k, :] for k in range(KC)]

                def merge(m, first):
                    at = pl["M"](m)
                    unit(at, 0, xh, xl)
                    if first:
                        cumulate(l * 24 + 21, l * 8 + 7)
                    unit(at, 1, xh, xl)
                    if first:
                        attend(l * 24 + 21, m0, (l + 1) * PAIRS, 1)
                        pe.wait_ge(ya_ok, l * KC + KC)
                        pe.wait_ge(yb_ok, l * KC + KC)
                    pe.wait_ge(yb_bank_free, l * KD + m + 1)
                    unit(at, 2, abh, abl, [bank[at.slot(2)], bank_yb])
                    if first:
                        pe.wait_ge(yc_ok, l * 8 + 8)
                    unit(at, 3, ch, cl, kc=KC)

                merge(0, True)
                with pe.Fori(1, KD) as m:
                    merge(m, False)

                mh = [mid_hi[:, k, :] for k in range(8)]
                ml = [mid_lo[:, k, :] for k in range(8)]
                mids = l * (KD + KF)
                with pe.Fori(0, 2) as i:
                    for c in range(4):
                        unit(pl["O"](i), c, mh, ml, ready=(mid_ok, mids) if c == 0 else None)

                def gate_up(p, i, first=False):
                    at = pl["GU"](p, i)
                    for c in range(4):
                        unit(at, c, xh, xl, ready=(xg_ok, l * (2 * KD) + KD) if first and c == 0 else None)
                        if first and c == 1:
                            row_squares(l * 2 + 2)

                for p, (f0, n) in enumerate(PARTS):
                    if p == 0:
                        gate_up(0, 0, True)
                    with pe.Fori(1 if p == 0 else 0, n // 2) as i:
                        gate_up(p, i)
                    with pe.Fori(0, 2) as i:
                        for c in range(4):
                            unit(pl["WD"](p, i), c, mh[:n], ml[:n], kc=n, k0=KD - n,
                                 ready=(mid_ok, mids + (KD + f0)) if c == 0 else None)

            for half in range(2):
                pe.wait_ge(x_new, KD + 2 * KD * L - KD // 2 * (1 - half))
                for n in range(NT):
                    for c in range(4):
                        last = nc.tensor.transpose(out_bank[half][n][:, c * P:(c + 1) * P],
                                                   xT[:, 4 * half + c, n * P:(n + 1) * P], ident[:, :])
                    last.then_inc((o_turned0, o_turned1)[half], 1)

        @block.scalar
        def _(act):
            af = nc.scalar.activation

            def split_hi(at, c, kc=KD):
                act.wait_ge(raw_full[at.slot(c)], at.round(c, 16))
                af(w_hi[at.slot(c)][:, 0:kc, :], raw[at.slot(c)][:, 0:kc, :], ACT.Copy).then_inc(hi_done, 1)

            def rms_chain(nth, src, count, freed=None):
                act.wait_ge(chain_done, nth + 1)
                op = af(N0[:, :], src[:, :], ACT.Identity, scale=1.0 / count, bias=eps[:, 0:1])
                if freed is not None:
                    op.then_inc(freed, 1)
                act.drain()
                af(N1[:, :], N0[:, :], ACT.Ln)
                act.drain()
                af(N1[:, :], N1[:, :], ACT.Exp, scale=-0.5)
                act.drain()
                af(N2, N1[:, :], ACT.Square).then_inc(chain, 1)

            def xg_round(n_new, c, gain):
                act.wait_ge(x_new, n_new)
                af(xg_hi[:, c, :], xT[:, c, :], ACT.Copy, scale=gain).then_inc(xg_hi_ok, 1)

            def q_round():
                for e in range(2):
                    own = slice(HD * e, HD * e + HD)
                    for rows in (slice(0, HD), slice(HD, P)):
                        last = af(q_twice[rows, e, :], QT[own, :], ACT.Copy)
                last.then_inc(qk_hi, 1)

            def k_round():
                for e in range(2):
                    own = slice(HD * e, HD * e + HD)
                    last = af(k_both[own, e, :], KT[own, :], ACT.Copy)
                last.then_inc(qk_hi, 1)

            def ln_exp_table():
                act.preload_act_table_set("natural_log_exp_and_others")

            def softplus_logs(h3):
                for g, (a, n) in enumerate(S_COLS):
                    act.wait_ge(z_done, h3 + (g + 1))
                    af(t_s[:, a:a + n], z[g][:, 0:n], ACT.Abs)
                act.drain()
                for g, (a, n) in enumerate(S_COLS):
                    af(t_s[:, a:a + n], t_s[:, a:a + n], ACT.Exp, scale=-1.0)
                act.drain()
                for g, (a, n) in enumerate(S_COLS):
                    af(t_s[:, a:a + n], t_s[:, a:a + n], ACT.Ln, bias=1.0).then_inc(z_ln, 1)

            def softplus_hi(h3):
                for g, (a, n) in enumerate(S_COLS):
                    act.wait_ge(sp_ok, h3 + (g + 1))
                    af(s_hi[:, a:a + n], t_s[:, a:a + n], ACT.Copy).then_inc(sp_hi, 1)

            def attention_exp(h3):
                for g, (a, n) in enumerate(S_COLS):
                    act.wait_ge(cum_done, h3 + (g + 1))
                    af(t_s[:, a:a + n], z[g][:, 0:n], ACT.Exp).then_inc(a_exp, 1)
                act.drain()
                for g, (a, n) in enumerate(S_COLS):
                    af(s_hi[:, a:a + n], t_s[:, a:a + n], ACT.Copy).then_inc(a_hi, 1)

            def yc_half(n_misc):
                act.wait_ge(misc_done, n_misc + 1)
                af(N1[0:HD, :], misc[HD:P, :], ACT.Copy).then_inc(yc_half_ok, 1)

            def yc_round(nth, j, e):
                rows = slice(HD * e, HD * e + HD)
                act.wait_ge(yc_sum, nth + 1)
                af(yc_hi[rows, bass.ds(j, 1), :].rearrange("p a t -> p (a t)"), N1[rows, :], ACT.Copy).then_inc(yc_hi_ok, 1)

            def ln_round(l, n):
                act.wait_ge(ln_pre, l * NT + n + 1)
                af(yb_hi[:, :, n * P:(n + 1) * P], (S0, S1)[n % 2][:, :].rearrange("p (g c) -> p g c", g=KC),
                   ACT.Copy).then_inc(ln_hi, 1)

            ln_exp_table()
            act.wait_ge(consts, 1)
            start = Units(0)
            act.wait_ge(par_ok, 1)
            for c in range(KD):
                act.wait_ge(x_turned, c + 1)
                af(xg_hi[:, c, :], bank[c % NB][:, :], ACT.Copy, scale=gain0[:, c:c + 1]).then_inc(xg_hi_ok, 1)
                af(xT[:, c, :], bank[c % NB][:, :], ACT.Copy).then_inc(x_new, 1)
                if c == KD - AHEAD:
                    split_hi(start, 0)
            for c in range(1, AHEAD):
                split_hi(start, c)

            with act.Fori(0, L) as l:
                pl = places(l)
                m0 = l * M_LAYER + 1
                at = pl["P"]
                nchain = l * CHAINS
                split_hi(at, 3)
                split_hi(at, 4)
                ln_exp_table()
                act.wait_ge(sq_done, l * 2 + 1)
                rms_chain(nchain, bank_sq, -D)
                for c in range(4):
                    act.wait_ge(sv_raw, l * 4 + c + 1)
                    af(gates[:, c, :], gates[:, c, :], ACT.Gelu).then_inc(sv_ok, 1)
                    if c >= 2:
                        split_hi(at, 3 + c)
                split_hi(at, 7)

                def keep_tokens(c, src):
                    return af(v_tok[:, :, c * P:(c + 1) * P], src[:, :].rearrange("p (n c) -> p n c", n=NT),
                              ACT.Copy)

                for c in range(3):
                    act.wait_ge(sv_turned, l * 3 + c + 1)
                    keep_tokens(c, sv_bank[c]).then_inc(sv_kept, 1)
                split_hi(at, 8)
                act.wait_ge(misc_done, m0 + 2)
                keep_tokens(3, misc).then_inc(sv_kept, 1)
                act.drain()
                act.sem_inc(misc_free, 1)
                ln_exp_table()
                act.wait_ge(ln_var, l + 1)
                af(ln_v[:, :], ln_mv[:, :, 1:2].rearrange("p n a -> p (n a)"), ACT.Identity, bias=eps[:, 0:1])
                act.drain()
                af(ln_r[:, :], ln_v[:, :], ACT.Ln)
                act.drain()
                af(ln_r[:, :], ln_r[:, :], ACT.Exp, scale=-0.5)
                act.drain()
                af(ln_t[:, :], ln_r[:, :], ACT.Square).then_inc(ln_chain, 1)
                act.wait_ge(misc_done, m0 + 3)
                rms_chain(nchain + 1, misc, HD, misc_free)
                split_hi(at, 9)
                act.wait_ge(qk_nrm, l * 8 + 1)
                q_round()
                act.wait_ge(misc_done, m0 + 4)
                rms_chain(nchain + 2, misc, HD, misc_free)
                ln_round(l, 0)
                act.wait_ge(qk_nrm, l * 8 + 2)
                k_round()
                split_hi(at, 10)
                ln_round(l, 1)
                ln_round(l, 2)
                split_hi(at, 11)
                act.wait_ge(misc_done, m0 + 5)
                af(sw_hi[:, :, :], misc[:, :].rearrange("p (g t) -> p g t", g=KC), ACT.Copy).then_inc(sw_hi_ok, 1)
                ln_round(l, 3)
                split_hi(at, 12)
                m0 = m0 + M_P

                def pair(j, last, m0):
                    at = pl["A"](j)
                    h3 = l * 24 + j * 6
                    pairs = l * PAIRS + j

                    def flat(t):
                        return t[:, bass.ds(j, 1), :].rearrange("p a t -> p (a t)")

                    def mix_slabs():
                        act.wait_ge(ln_ok, l * 4 + 4)
                        act.wait_ge(misc_done, m0 - 1)
                        for dst, src in ((mix_hi, yb_hi), (mix_lo, yb_lo)):
                            act.dma_start(dst[:, :, :].bitcast(F32),
                                          src[:, bass.ds(j, 1), :].rearrange("p a (n c) -> p (a n) c", n=NT).bitcast(F32)
                                          ).then_inc(slab_in, 16)

                    def ya_round():
                        act.wait_ge(ya_pre, pairs + 1)
                        af(flat(ya_hi), S1[:, :], ACT.Copy).then_inc(ya_hi_ok, 1)

                    def gelu_u():
                        act.wait_ge(u_raw, pairs + 1)
                        af(S2[:, :], S2[:, :], ACT.Gelu).then_inc(u_ok, 1)

                    def yb_round():
                        act.wait_ge(yb_pre, pairs + 1)
                        act.sem_inc(passed, 1)
                        af(flat(yb_hi), N0[:, :], ACT.Copy).then_inc(yb_hi_ok, 1)

                    softplus_logs(h3)
                    softplus_hi(h3)
                    split_hi(at, 3)
                    mix_slabs()
                    split_hi(at, 4)
                    act.wait_ge(misc_done, m0 + 1)
                    af(v_both[:, :, 0, :], misc[:, :].rearrange("p (n c) -> p n c", c=HD), ACT.Copy).then_inc(v_hi_ok, 1)
                    split_hi(at, 5)
                    attention_exp(h3)
                    if last:
                        split_hi(at, 6)
                        yc_half(m0 + 1)
                        softplus_logs(h3 + 3)
                        yc_round(l * 8 + j * 2, j, 0)
                        split_hi(at, 7)
                        softplus_hi(h3 + 3)
                        ya_round()
                        split_hi(at, 8)
                        gelu_u()
                        yb_round()
                        ln_exp_table()
                        return
                    nch = l * CHAINS + (j * 2 + 3)
                    act.wait_ge(misc_done, m0 + 2)
                    rms_chain(nch, misc, HD, misc_free)
                    split_hi(at, 6)
                    act.wait_ge(qk_nrm, l * 8 + (j * 2 + 3))
                    yc_half(m0 + 2)
                    softplus_logs(h3 + 3)
                    yc_round(l * 8 + j * 2, j, 0)
                    q_round()
                    split_hi(at, 7)
                    softplus_hi(h3 + 3)
                    act.wait_ge(misc_done, m0 + 4)
                    act.wait_ge(yc_ok, l * 8 + (j * 2 + 1))
                    rms_chain(nch + 1, misc, HD, misc_free)
                    split_hi(at, 8)
                    act.wait_ge(qk_nrm, l * 8 + (j * 2 + 4))
                    k_round()
                    split_hi(at, 9)
                    attention_exp(h3 + 3)
                    ya_round()
                    gelu_u()
                    split_hi(at, 10)
                    yb_round()
                    ln_exp_table()
                    yc_half(m0 + 5)
                    yc_round(l * 8 + (j * 2 + 1), j, 1)

                ln_exp_table()
                with act.Fori(0, PAIRS - 1) as j:
                    pair(j, False, m0 + j * M_PAIR)
                m0 = m0 + (PAIRS - 1) * M_PAIR
                pair(PAIRS - 1, True, m0)
                m0 = m0 + M_PAIR_LAST

                act.wait_ge(ya_ok, l * KC + KC)
                act.wait_ge(par_ok, l + 2)

                def merge(m, first):
                    at = pl["M"](m)
                    nm = l * KD + m

                    def sigmoid(s, gate, bias):
                        af(s[:, :], gate, ACT.Sigmoid, bias=par[:, bass.ds(m + (R_BG + bias * KD), 1)]).then_inc(g_sig, 1)

                    split_hi(at, 3, KC)
                    if first:
                        attention_exp(l * 24 + 21)
                        split_hi(at, 4)
                    act.wait_ge(merged, nm + 1)
                    sigmoid(S0, gates[:, bass.ds(m, 1), :].rearrange("p a t -> p (a t)"), 0)
                    act.wait_ge(g_raw, nm * 2 + 1)
                    sigmoid(S1, S1[:, :], 1)
                    if not first:
                        split_hi(at, 4)
                    act.wait_ge(g_raw, nm * 2 + 2)
                    sigmoid(S2, S2[:, :], 2)
                    if first:
                        yc_half(m0)
                        yc_round(l * 8 + 7, PAIRS - 1, 1)
                    split_hi(at, 5)
                    split_hi(at, 6)
                    act.wait_ge(merged, nm + 2)
                    af(mid_hi[:, bass.ds(m, 1), :].rearrange("p a t -> p (a t)"), N0[:, :], ACT.Copy).then_inc(mid_hi_ok, 1)

                merge(0, True)
                with act.Fori(1, KD) as m:
                    merge(m, False)

                with act.Fori(0, 2) as i:
                    for c in range(4):
                        split_hi(pl["O"](i), c + 3)
                        xg_round(l * (2 * KD) + (i * 4 + (KD + c + 1)), bass.ds(i * 4 + c, 1),
                                 par[:, bass.ds(i * 4 + (R_GF + c), 1)])

                def gate_up(p, i, first=False):
                    at = pl["GU"](p, i)
                    f0 = PARTS[p][0]
                    for c in range(4):
                        f = i * 2 + c // 2
                        nf = l * KF + f0 + f
                        if not (first and c == 1):
                            split_hi(at, c + 3)
                        if first and c == 0:
                            split_hi(at, 4)
                            ln_exp_table()
                            act.wait_ge(sq_done, l * 2 + 2)
                            rms_chain(l * CHAINS + (CHAINS - 1), bank_sq, -D)
                        if c % 2 == 0:
                            act.wait_ge(silu_in, nf + 1)
                            af(S0[:, :], S0[:, :], ACT.Silu).then_inc(silu_ok, 1)
                        else:
                            act.wait_ge(act_pre, nf + 1)
                            af(mid_hi[:, bass.ds(f, 1), :].rearrange("p a t -> p (a t)"), N0[:, :], ACT.Copy
                               ).then_inc(mid_hi_ok, 1)

                for p, (f0, n) in enumerate(PARTS):
                    if p == 0:
                        gate_up(0, 0, True)
                    with act.Fori(1 if p == 0 else 0, n // 2) as i:
                        gate_up(p, i)
                    with act.Fori(0, 2) as i:
                        for c in range(4):
                            split_hi(pl["WD"](p, i), c + 3)
                            if p == len(PARTS) - 1:
                                xg_round(l * (2 * KD) + (i * 4 + (2 * KD + c + 1)), bass.ds(i * 4 + c, 1),
                                         par[:, bass.ds(i * 4 + (R_GM + c), 1)])

            for n in range(NT):
                act.wait_ge(o_turned0, n + 1)
                af(toks[:, n, 0:T], out_bank[0][n][:, :], ACT.Copy).then_inc(o_act, 1)

        @block.vector
        def _(dve):
            tt, ts, stt = nc.vector.tensor_tensor, nc.vector.tensor_scalar, nc.vector.scalar_tensor_tensor
            copy = nc.vector.tensor_copy

            def split_lo(at, c, kc=KD):
                dve.wait_ge(hi_done, at.count(c))
                r, h, w = raw[at.slot(c)], w_hi[at.slot(c)], w_lo[at.slot(c)]
                tt(w[:, 0:kc, :], r[:, 0:kc, :], h[:, 0:kc, :].bitcast(F32), ALU.subtract).then_inc(lo_done, 1)

            def scaled(at, c, dst):
                dve.wait_ge(unit_done, at.count(c, RAW))
                return tt(dst, bank[at.slot(c)][:, :], rstd[:, :], ALU.mult).then_inc(bank_free[at.slot(c)], 1)

            def newton(nth, dst):
                dve.wait_ge(chain, nth + 1)
                stt(N2, N0[:, :], -0.5, N2, ALU.mult, ALU.mult)
                dve.drain()
                stt(dst, N2, 1.5, N1[:, :], ALU.add, ALU.mult).then_inc(chain_done, 1)
                dve.drain()

            def softplus_sum(h3):
                for g, (a, n) in enumerate(S_COLS):
                    dve.wait_ge(z_ln, h3 + (g + 1))
                    stt(t_s[:, a:a + n], z[g][:, 0:n], 0.0, t_s[:, a:a + n], ALU.max, ALU.add).then_inc(sp_ok, 1)

            def softplus_lo(h3):
                for g, (a, n) in enumerate(S_COLS):
                    dve.wait_ge(sp_hi, h3 + (g + 1))
                    tt(s_lo[:, a:a + n], t_s[:, a:a + n], s_hi[:, a:a + n].bitcast(F32), ALU.subtract).then_inc(sp_lo, 1)

            def attention_lo(h3):
                for g, (a, n) in enumerate(S_COLS):
                    dve.wait_ge(a_hi, h3 + (g + 1))
                    tt(s_lo[:, a:a + n], t_s[:, a:a + n], s_hi[:, a:a + n].bitcast(F32), ALU.subtract).then_inc(a_lo, 1)

            def yc_add(nth, e):
                dve.wait_ge(yc_half_ok, nth + 1)
                tt(N1[HD * e:HD * e + HD, :], N1[0:HD, :], misc[0:HD, :], ALU.add).then_inc(yc_sum, 1)
                dve.drain()
                dve.sem_inc(misc_free, 1)

            def yc_rest(nth, j, e):
                rows = slice(HD * e, HD * e + HD)
                dve.wait_ge(yc_hi_ok, nth + 1)
                flat = lambda t: t[rows, bass.ds(j, 1), :].rearrange("p a t -> p (a t)")
                tt(flat(yc_lo), N1[rows, :], flat(yc_hi).bitcast(F32), ALU.subtract).then_inc(yc_ok, 1)

            def head_norm(nth_chain, s, gain):
                newton(nth_chain, N1[:, :])
                stt(s[:, :], s[:, :], gain, N1[:, :], ALU.mult, ALU.mult).then_inc(qk_nrm, 1)

            def q_rest(n_qk):
                dve.wait_ge(qk_hi, n_qk)
                for e in range(2):
                    own = slice(HD * e, HD * e + HD)
                    last = tt(q_lo[own, :], QT[own, :], q_twice[own, e, :].bitcast(F32), ALU.subtract)
                last.then_inc(q_ok, 1)

            dve.sem_inc(unit_done, RAW)
            dve.sem_inc(a_exp, 3)
            dve.sem_inc(merged, 1)
            for s in (chain_done, misc_free, yb_bank_free):
                dve.sem_inc(s, 1)
            nc.vector.memset(eps[:, :], EPS)
            nc.vector.memset(conv_in[:, 0:2], 0.0)
            nc.vector.memset(N1[:, 0:P], 0.0)
            nc.vector.memset(N0[:, 0:P], -1.0)
            dve.drain()
            nc.vector.memset(N1[0:HD, 0:HD], 1.0)
            nc.vector.memset(N1[HD:P, HD:P], 1.0)
            dve.wait_ge(ident_ok, 1)
            copy(ident_r[:, :], ident[:, :])
            copy(neg_tri[:, :], S0[:, 0:P])
            copy(mask_add[:, :], S1[:, 0:P])
            copy(neg_ones[:, :], N0[:, 0:P])
            dve.drain()
            copy(head_ones[:, :], N1[:, 0:P])
            dve.drain()
            dve.sem_inc(consts, 1)

            dve.wait_ge(misc_done, 1)
            copy(gain0[:, :], misc[:, 0:KD]).then_inc(par_ok, 1)
            dve.drain()
            dve.sem_inc(misc_free, 1)
            for c in range(KD):
                dve.wait_ge(x_new, c + 1)
                stt(xg_lo[:, c, :], bank[c % NB][:, :], gain0[:, c:c + 1], xg_hi[:, c, :].bitcast(F32),
                    ALU.mult, ALU.subtract).then_inc(xg_ok, 1)
                if c >= KD - NB:
                    dve.drain()
                    dve.sem_inc(bank_free[c % NB], 1)
            start = Units(0)
            for c in range(AHEAD):
                split_lo(start, c)

            with dve.Fori(0, L) as l:
                pl = places(l)
                m0 = l * M_LAYER + 1
                at = pl["P"]
                nchain = l * CHAINS
                def layer_norm(n):
                    e = (S0, S1)[n % 2]
                    if n >= 2:
                        dve.drain()
                    stt(e[:, :], v_tok[:, n, :], ln_mv[:, n, 0:1], ln_g[:, :], ALU.subtract, ALU.mult)
                    dve.drain()
                    stt(e[:, :], e[:, :], ln_rstd[:, n:n + 1], ln_b[:, :], ALU.mult, ALU.add).then_inc(ln_pre, 1)

                def layer_norm_lo(n):
                    dve.wait_ge(ln_hi, l * 4 + n + 1)
                    tt(yb_lo[:, :, n * P:(n + 1) * P], (S0, S1)[n % 2][:, :].rearrange("p (g c) -> p g c", g=KC),
                       yb_hi[:, :, n * P:(n + 1) * P].bitcast(F32), ALU.subtract).then_inc(ln_ok, 1)

                split_lo(at, 3)
                split_lo(at, 4)
                newton(nchain, rstd[:, :])
                for c in range(4):
                    scaled(at, c, gates[:, c, :])
                    dve.drain()
                    dve.sem_inc(sv_raw, 1)
                    if c >= 2:
                        split_lo(at, c + 3)
                dve.wait_ge(misc_done, m0 + 1)
                copy(par[:, 0:NPAR], misc[:, 0:NPAR])
                dve.drain()
                ts(par[:, R_GQ:R_GQ + 1], par[:, R_GQ:R_GQ + 1], HD ** -0.5, None, ALU.mult)
                dve.drain()
                dve.sem_inc(par_ok, 1)
                dve.sem_inc(misc_free, 1)
                scaled(at, 4, QT[:, :])
                dve.drain()
                dve.sem_inc(qk_raw, 1)
                split_lo(at, 7)
                scaled(at, 5, KT[:, :])
                dve.drain()
                dve.sem_inc(qk_raw, 1)
                dve.wait_ge(sv_kept, l * 4 + 4)
                for n in range(NT):
                    nc.vector.bn_stats(ln_stats[:, n, :], v_tok[:, n, :])
                dve.drain()
                for n in range(NT):
                    nc.vector.bn_aggr(ln_mv[:, n, :], ln_stats[:, n, :])
                dve.drain()
                dve.sem_inc(ln_var, 1)
                split_lo(at, 8)
                scaled(at, 6, gates[:, 4, :])
                dve.wait_ge(ln_chain, l + 1)
                stt(ln_t[:, :], ln_v[:, :], -0.5, ln_t[:, :], ALU.mult, ALU.mult)
                dve.drain()
                stt(ln_rstd[:, :], ln_t[:, :], 1.5, ln_r[:, :], ALU.add, ALU.mult)
                dve.drain()
                head_norm(nchain + 1, QT, par[:, R_GQ:R_GQ + 1])
                split_lo(at, 9)
                dve.wait_ge(ln_in, l * 48 + 48)
                layer_norm(0)
                q_rest(l * 8 + 1)
                scaled(at, 7, gates[:, 5, :])
                head_norm(nchain + 2, KT, par[:, R_GK:R_GK + 1])
                layer_norm(1)
                layer_norm_lo(0)
                split_lo(at, 10)
                layer_norm(2)
                scaled(at, 8, gates[:, 6, :])
                layer_norm_lo(1)
                layer_norm(3)
                split_lo(at, 11)
                dve.wait_ge(sw_hi_ok, l + 1)
                tt(sw_lo[:, :, :], misc[:, :].rearrange("p (g t) -> p g t", g=KC), sw_hi[:, :, :].bitcast(F32),
                   ALU.subtract)
                dve.drain()
                dve.sem_inc(misc_free, 1)
                scaled(at, 9, gates[:, 7, :])
                layer_norm_lo(2)
                layer_norm_lo(3)
                split_lo(at, 12)
                m0 = m0 + M_P

                def pair(j, last, m0):
                    at = pl["A"](j)
                    h3 = l * 24 + j * 6
                    pairs = l * PAIRS + j
                    j1 = bass.ds(j, 1)

                    def flat(t):
                        return t[:, j1, :].rearrange("p a t -> p (a t)")

                    def tap(k):
                        return par[:, bass.ds(j + (R_CW + 4 * k), 1)]

                    def convolution():
                        dve.drain()
                        tt(conv_in[:, 2:2 + T], S1[:, :], S2[:, :], ALU.mult)
                        dve.drain()
                        ts(S1[:, :], conv_in[:, 2:2 + T], tap(2), par[:, bass.ds(j + R_CB, 1)], ALU.mult, ALU.add)
                        dve.drain()
                        stt(S1[:, :], conv_in[:, 1:1 + T], tap(1), S1[:, :], ALU.mult, ALU.add)
                        dve.drain()
                        stt(S1[:, :], conv_in[:, 0:T], tap(0), S1[:, :], ALU.mult, ALU.add)
                        dve.drain()
                        tt(S1[:, :], S1[:, :], S0[:, :], ALU.mult).then_inc(ya_pre, 1)

                    def ya_rest():
                        dve.wait_ge(ya_hi_ok, pairs + 1)
                        tt(flat(ya_lo), S1[:, :], flat(ya_hi).bitcast(F32), ALU.subtract).then_inc(ya_ok, 1)

                    def yb_rest():
                        dve.wait_ge(yb_hi_ok, pairs + 1)
                        tt(flat(yb_lo), N0[:, :], flat(yb_hi).bitcast(F32), ALU.subtract).then_inc(yb_ok, 1)

                    def v_rest():
                        dve.wait_ge(v_hi_ok, pairs + 1)
                        tt(v_both[:, :, 1, :], misc[:, :].rearrange("p (n c) -> p n c", c=HD), v_both[:, :, 0, :].bitcast(F32),
                           ALU.subtract).then_inc(v_ok, 1)
                        dve.drain()
                        dve.sem_inc(misc_free, 1)

                    scaled(at, 0, N0[:, :])
                    dve.drain()
                    dve.sem_inc(v_raw, 1)
                    softplus_sum(h3)
                    softplus_lo(h3)
                    if last:
                        split_lo(at, 3)
                        scaled(at, 1, S0[:, :])
                        split_lo(at, 4)
                        v_rest()
                        scaled(at, 2, S1[:, :])
                        split_lo(at, 5)
                        attention_lo(h3)
                        scaled(at, 3, S2[:, :])
                        split_lo(at, 6)
                        yc_add(l * 8 + j * 2, 0)
                        softplus_sum(h3 + 3)
                        yc_rest(l * 8 + j * 2, j, 0)
                        convolution()
                        softplus_lo(h3 + 3)
                        scaled(at, 4, S2[:, :])
                        dve.drain()
                        dve.sem_inc(u_raw, 1)
                        ya_rest()
                        split_lo(at, 7)
                        mixed(m0 + 2, j1)
                        with_u(pairs)
                        split_lo(at, 8)
                        yb_rest()
                        return
                    scaled(at, 1, QT[:, :])
                    dve.drain()
                    dve.sem_inc(qk_raw, 1)
                    split_lo(at, 3)
                    split_lo(at, 4)
                    v_rest()
                    dve.wait_ge(k_ok, pairs + 1)
                    scaled(at, 2, KT[:, :])
                    dve.drain()
                    dve.sem_inc(qk_raw, 1)
                    split_lo(at, 5)
                    attention_lo(h3)
                    nch = l * CHAINS + (j * 2 + 3)
                    head_norm(nch, QT, par[:, R_GQ:R_GQ + 1])
                    scaled(at, 3, S0[:, :])
                    split_lo(at, 6)
                    yc_add(l * 8 + j * 2, 0)
                    softplus_sum(h3 + 3)
                    yc_rest(l * 8 + j * 2, j, 0)
                    q_rest(l * 8 + (j * 2 + 3))
                    scaled(at, 4, S1[:, :])
                    split_lo(at, 7)
                    softplus_lo(h3 + 3)
                    head_norm(nch + 1, KT, par[:, R_GK:R_GK + 1])
                    scaled(at, 5, S2[:, :])
                    split_lo(at, 8)
                    mixed(m0 + 4, j1)
                    split_lo(at, 9)
                    convolution()
                    attention_lo(h3 + 3)
                    scaled(at, 6, S2[:, :])
                    dve.drain()
                    dve.sem_inc(u_raw, 1)
                    ya_rest()
                    scaled(at, 7, flat(gates))
                    with_u(pairs)
                    split_lo(at, 10)
                    yb_rest()
                    yc_add(l * 8 + (j * 2 + 1), 1)
                    yc_rest(l * 8 + (j * 2 + 1), j, 1)

                def mixed(n_misc, j1):
                    dve.wait_ge(misc_done, n_misc + 1)
                    b = sgu_bias[:, j1, :].broadcast_to([P, NT, P])
                    tt(N0[:, :].rearrange("p (n t) -> p n t", n=NT), misc[:, :].rearrange("p (n t) -> p n t", n=NT),
                       b, ALU.add).then_inc(misc_free, 1)

                def with_u(pairs):
                    dve.drain()
                    dve.wait_ge(u_ok, pairs + 1)
                    tt(N0[:, :], N0[:, :], S2[:, :], ALU.mult).then_inc(yb_pre, 1)

                with dve.Fori(0, PAIRS - 1) as j:
                    pair(j, False, m0 + j * M_PAIR)
                m0 = m0 + (PAIRS - 1) * M_PAIR
                pair(PAIRS - 1, True, m0)
                m0 = m0 + M_PAIR_LAST

                def merge(m, first):
                    at = pl["M"](m)
                    nm = l * KD + m
                    m1 = bass.ds(m, 1)
                    scaled(at, 0, S1[:, :])
                    dve.drain()
                    dve.sem_inc(g_raw, 1)
                    split_lo(at, 3, KC)
                    if first:
                        attention_lo(l * 24 + 21)
                        split_lo(at, 4)
                        scaled(pl["A"](PAIRS - 1), 5, gates[:, PAIRS - 1, :])
                    scaled(at, 1, S2[:, :])
                    dve.drain()
                    dve.sem_inc(g_raw, 1)
                    if first:
                        yc_add(l * 8 + 7, 1)
                        yc_rest(l * 8 + 7, PAIRS - 1, 1)
                        dve.drain()
                    else:
                        split_lo(at, 4)
                    dve.wait_ge(g_sig, nm * 3 + 2)
                    dve.wait_ge(unit_done, at.count(2, RAW))
                    tt(N0[:, :], bank[at.slot(2)][:, :], S0[:, :], ALU.mult).then_inc(bank_free[at.slot(2)], 1)
                    tt(N1[:, :], bank_yb[:, :], S1[:, :], ALU.mult).then_inc(yb_bank_free, 1)
                    dve.drain()
                    tt(N0[:, :], N0[:, :], N1[:, :], ALU.add)
                    split_lo(at, 5)
                    dve.drain()
                    dve.wait_ge(g_sig, nm * 3 + 3)
                    dve.wait_ge(unit_done, at.count(3, RAW))
                    tt(N1[:, :], bank[at.slot(3)][:, :], S2[:, :], ALU.mult).then_inc(bank_free[at.slot(3)], 1)
                    dve.drain()
                    tt(N0[:, :], N0[:, :], N1[:, :], ALU.add).then_inc(merged, 1)
                    dve.wait_ge(mid_hi_ok, l * (KD + KF) + m + 1)
                    tt(mid_lo[:, m1, :].rearrange("p a t -> p (a t)"), N0[:, :],
                       mid_hi[:, m1, :].rearrange("p a t -> p (a t)").bitcast(F32), ALU.subtract).then_inc(mid_ok, 1)
                    split_lo(at, 6)

                merge(0, True)
                with dve.Fori(1, KD) as m:
                    merge(m, False)

                def renew(at, c, i, prep, gain_row=0, news=0):
                    dve.wait_ge(unit_done, at.count(c, RAW))
                    xc = bass.ds(i * 4 + c, 1)
                    xs = xT[:, xc, :].rearrange("p a t -> p (a t)")
                    tt(xs, xs, bank[at.slot(c)][:, :], ALU.add).then_inc(bank_free[at.slot(c)], 1)
                    if prep:
                        dve.drain()
                        dve.sem_inc(x_new, 1)
                        dve.wait_ge(xg_hi_ok, news + (i * 4 + (c + 1)))
                        stt(xg_lo[:, xc, :].rearrange("p a t -> p (a t)"), xs, par[:, bass.ds(i * 4 + (gain_row + c), 1)],
                            xg_hi[:, xc, :].rearrange("p a t -> p (a t)").bitcast(F32), ALU.mult, ALU.subtract
                            ).then_inc(xg_ok, 1)

                with dve.Fori(0, 2) as i:
                    at = pl["O"](i)
                    for c in range(4):
                        renew(at, c, i, True, R_GF, l * (2 * KD) + KD)
                        split_lo(at, c + 3)

                def gate_up(p, i, first=False):
                    at = pl["GU"](p, i)
                    f0 = PARTS[p][0]
                    for c in range(4):
                        f = i * 2 + c // 2
                        nf = l * KF + f0 + f
                        f1 = bass.ds(f, 1)
                        if first and c == 0:
                            split_lo(at, 3)
                            split_lo(at, 4)
                            newton(l * CHAINS + (CHAINS - 1), rstd[:, :])
                        if c % 2 == 0:
                            scaled(at, c, S0[:, :])
                            dve.drain()
                            dve.sem_inc(silu_in, 1)
                        else:
                            scaled(at, c, S1[:, :])
                            dve.drain()
                            dve.wait_ge(silu_ok, nf + 1)
                            tt(N0[:, :], S0[:, :], S1[:, :], ALU.mult).then_inc(act_pre, 1)
                            dve.wait_ge(mid_hi_ok, l * (KD + KF) + (KD + f0) + f + 1)
                            tt(mid_lo[:, f1, :].rearrange("p a t -> p (a t)"), N0[:, :],
                               mid_hi[:, f1, :].rearrange("p a t -> p (a t)").bitcast(F32), ALU.subtract
                               ).then_inc(mid_ok, 1)
                        if not (first and c <= 1):
                            split_lo(at, c + 3)

                for p, (f0, n) in enumerate(PARTS):
                    if p == 0:
                        gate_up(0, 0, True)
                    with dve.Fori(1 if p == 0 else 0, n // 2) as i:
                        gate_up(p, i)
                    with dve.Fori(0, 2) as i:
                        at = pl["WD"](p, i)
                        for c in range(4):
                            renew(at, c, i, p == len(PARTS) - 1, R_GM, l * (2 * KD) + 2 * KD)
                            split_lo(at, c + 3)

            for n in range(NT):
                dve.wait_ge(o_turned1, n + 1)
                copy(toks[:, n, T:2 * T], out_bank[1][n][:, :]).then_inc(o_dve, 1)


def kernel(**inputs):
    import numpy as np
    import concourse.bacc as bacc
    from concourse.bass_utils import run_bass_kernel_spmd

    names = ["x", "mix_norm_g", "w_in", "b_gate", "conv_w", "conv_b", "sgu_ln_g", "sgu_ln_b", "sgu_w", "sgu_b",
             "q_norm_g", "k_norm_g", "w_branch_out", "w_o", "ffn_norm_g", "w_gate_up", "w_down"]
    nc = bacc.Bacc("TRN2", target_bir_lowering=False, num_devices=1)
    arrays, args = {}, []
    for name in names:
        a = np.ascontiguousarray(inputs[name])
        arrays[f"in_{name}"] = a
        args.append(nc.dram_tensor(f"in_{name}", a.shape, mybir.dt.from_np(a.dtype), kind="ExternalInput").ap())
    out = nc.dram_tensor("out_x", (1, T, D), F32, kind="ExternalOutput").ap()
    build(nc, *args, out)
    got = run_bass_kernel_spmd(nc, [arrays], core_ids=[0])
    return got.results[0]["out_x"]
```
